# Optimizing a Trainium2 kernel written in Bass

```python
import jax, jax.numpy as jnp
from jax import lax
import numpy as np

D_MODEL = 2048
BATCH = 1
SEQ = 1024
DEPTH = 1

D_MIX = D_MODEL
D_HGRN = D_MIX // 2
D_GLA = D_MIX - D_HGRN
HGRN_DK = 128
HGRN_HEADS = D_HGRN // HGRN_DK
HGRN_DV = D_HGRN // HGRN_HEADS
GLA_HEADS = 4
GLA_DK_TOTAL = D_GLA // 2
GLA_DK = GLA_DK_TOTAL // GLA_HEADS
GLA_DV = D_GLA // GLA_HEADS
GLA_GATE_RANK = 16
GLA_GATE_TAU = 16.0
PLE_DIM = 256
CHUNK = 64
EPS = 1e-6

IN_SPLITS = [D_HGRN, D_HGRN, D_HGRN, D_HGRN,
             GLA_DK_TOTAL, GLA_DK_TOTAL, D_GLA, D_GLA,
             GLA_GATE_RANK]
D_IN = sum(IN_SPLITS)

kernel_name = "hgrn2_gla_parallel_heads_ple"

def rms_norm(x, w):
    xf = x.astype(jnp.float32)
    y = xf * lax.rsqrt(jnp.mean(xf * xf, axis=-1, keepdims=True) + EPS)
    return (y * w.astype(jnp.float32)).astype(x.dtype)

def chunk_gated_linear_attention(q, k, v, log_g, scale):
    B, T, H, dk = q.shape
    dv = v.shape[-1]
    n = T // CHUNK

    def to_chunks(a):
        a = a.astype(jnp.float32).reshape(B, n, CHUNK, H, a.shape[-1])
        return jnp.transpose(a, (1, 0, 3, 2, 4))

    qc, kc, vc, gc = to_chunks(q * scale), to_chunks(k), to_chunks(v), to_chunks(log_g)
    causal = jnp.tril(jnp.ones((CHUNK, CHUNK), dtype=bool))[:, :, None]

    def step(S, inp):
        q_c, k_c, v_c, g_c = inp
        b = jnp.cumsum(g_c, axis=2)
        diff = b[:, :, :, None, :] - b[:, :, None, :, :]
        decay = jnp.where(causal, jnp.exp(jnp.where(causal, diff, 0.0)), 0.0)
        attn = jnp.einsum('bhik,bhjk,bhijk->bhij', q_c, k_c, decay)
        o = (jnp.einsum('bhij,bhjv->bhiv', attn, v_c)
             + jnp.einsum('bhik,bhkv->bhiv', q_c * jnp.exp(b), S))
        b_last = b[:, :, -1:, :]
        S = (jnp.exp(b_last[:, :, 0, :])[..., None] * S
             + jnp.einsum('bhjk,bhjv->bhkv', k_c * jnp.exp(b_last - b), v_c))
        return S, o

    S0 = jnp.zeros((B, H, dk, dv), jnp.float32)
    _, o = lax.scan(step, S0, (qc, kc, vc, gc))
    return jnp.transpose(o, (1, 0, 3, 2, 4)).reshape(B, T, H, dv)

def head_readout(o, norm_w, gate, n_heads, dv, dtype):
    B, T = o.shape[:2]
    o = rms_norm(o, norm_w.reshape(n_heads, dv))
    g = jax.nn.silu(gate.astype(jnp.float32)).reshape(B, T, n_heads, dv)
    return (o * g).reshape(B, T, n_heads * dv).astype(dtype)

def setup_inputs(seed: int = 0) -> dict:
    key = jax.random.key(seed)
    ks = jax.random.split(key, 16)
    f32 = jnp.float32
    nrm = lambda k, shape, s: (jax.random.normal(k, shape, f32) * s)
    gain = lambda k, shape: 1.0 + 0.02 * jax.random.normal(k, shape, f32)
    return {
        "x": jax.random.normal(ks[0], (BATCH, SEQ, D_MODEL), f32),
        "p": jax.random.normal(ks[1], (DEPTH, BATCH, SEQ, PLE_DIM), f32),
        "norm_mix_w": gain(ks[2], (DEPTH, D_MODEL)),
        "w_in": nrm(ks[3], (DEPTH, D_MODEL, D_IN), D_MODEL ** -0.5),
        "hgrn_lb": nrm(ks[4], (DEPTH + 1, D_HGRN), 0.1),
        "gla_gate_w2": nrm(ks[5], (DEPTH, GLA_GATE_RANK, GLA_DK_TOTAL), GLA_GATE_RANK ** -0.5),
        "gla_gate_b": nrm(ks[6], (DEPTH, GLA_DK_TOTAL), 0.01),
        "hgrn_norm_w": gain(ks[7], (DEPTH, D_HGRN)),
        "gla_norm_w": gain(ks[8], (DEPTH, D_GLA)),
        "w_out": nrm(ks[9], (DEPTH, D_MIX, D_MODEL), D_MIX ** -0.5),
        "ple_proj": nrm(ks[10], (DEPTH, PLE_DIM, D_MODEL), PLE_DIM ** -0.5),
        "ple_norm_w": gain(ks[11], (DEPTH, D_MODEL)),
        "ple_gate_norm_w": gain(ks[12], (DEPTH, D_MODEL)),
        "ple_gate_w": nrm(ks[13], (DEPTH, D_MODEL, D_MODEL), D_MODEL ** -0.5),
        "ple_gate_b": nrm(ks[14], (DEPTH, D_MODEL), 0.01),
        "final_norm_w": gain(ks[15], (D_MODEL,)),
    }

def reference(x, p, norm_mix_w, w_in, hgrn_lb, gla_gate_w2, gla_gate_b, hgrn_norm_w,
              gla_norm_w, w_out, ple_proj, ple_norm_w, ple_gate_norm_w, ple_gate_w,
              ple_gate_b, final_norm_w):
    B, T, _ = x.shape
    dtype = x.dtype
    lb_all = jnp.cumsum(jax.nn.softmax(hgrn_lb.astype(jnp.float32), axis=0), axis=0)
    offsets = np.cumsum(IN_SPLITS)[:-1].tolist()
    h = x
    for i in range(DEPTH):
        u = rms_norm(h, norm_mix_w[i])
        proj = u @ w_in[i]
        hq, hf, hi, hz, gq, gk, gv, gz, glr = jnp.split(proj, offsets, axis=-1)

        lb = lb_all[i]
        f = lb + (1.0 - lb) * jax.nn.sigmoid(hf.astype(jnp.float32))
        hshape = (B, T, HGRN_HEADS, HGRN_DK)
        o_h = chunk_gated_linear_attention(
            jax.nn.silu(hq.astype(jnp.float32)).reshape(hshape),
            (1.0 - f).reshape(hshape),
            hi.reshape(B, T, HGRN_HEADS, HGRN_DV),
            jnp.log(f).reshape(hshape),
            HGRN_DK ** -0.5)
        y_h = head_readout(o_h, hgrn_norm_w[i], hz, HGRN_HEADS, HGRN_DV, dtype)

        gate_logit = glr.astype(jnp.float32) @ gla_gate_w2[i].astype(jnp.float32) + gla_gate_b[i]
        log_a = jax.nn.log_sigmoid(gate_logit) / GLA_GATE_TAU
        gshape = (B, T, GLA_HEADS, GLA_DK)
        o_g = chunk_gated_linear_attention(
            gq.reshape(gshape), gk.reshape(gshape),
            gv.reshape(B, T, GLA_HEADS, GLA_DV), log_a.reshape(gshape),
            GLA_DK ** -0.5)
        y_g = head_readout(o_g, gla_norm_w[i], gz, GLA_HEADS, GLA_DV, dtype)

        y = jnp.concatenate([y_h, y_g], axis=-1) @ w_out[i]
        h = h + y.astype(dtype)

        e = rms_norm(p[i] @ ple_proj[i], ple_norm_w[i])
        gate = jax.nn.sigmoid(rms_norm(h, ple_gate_norm_w[i]) @ ple_gate_w[i] + ple_gate_b[i])
        h = h + (gate * e).astype(dtype)
    return rms_norm(h, final_norm_w)


_drawn_inputs = setup_inputs


def setup_inputs(seed=0):
    import zlib

    import numpy as np

    out = dict(_drawn_inputs(seed))
    spreads = {}
    factors = {'norm_mix_w': 3.28,
     'hgrn_lb': 8.0,
     'gla_gate_b': 30.002,
     'hgrn_norm_w': 86.989,
     'gla_norm_w': 91.462,
     'ple_norm_w': 200.0,
     'ple_gate_norm_w': 64.0,
     'ple_gate_b': 200.0,
     'final_norm_w': 20.712}
    for name, (base, spread) in spreads.items():
        noise = np.random.default_rng([zlib.crc32(name.encode()), seed]).standard_normal(out[name].shape)
        drawn = base * np.exp(spread * noise) if base else spread * noise
        out[name] = __import__('jax').numpy.asarray(drawn.astype(out[name].dtype))
    for name, factor in factors.items():
        out[name] = (out[name] * factor).astype(out[name].dtype)
    return out
```

```python
from contextlib import ExitStack

import numpy as np
import concourse.bass as bass
from concourse import mybir

F32 = mybir.dt.float32
F32R = mybir.dt.float32r
U8 = mybir.dt.uint8
ALU = mybir.AluOpType
ACT = mybir.ActivationFunctionType
AX = mybir.AxisListType

P = 128
SEQ, D = 1024, 2048
KT = D // P
HALVES = 2
TH = SEQ // HALVES
C = 128
NC_ = TH // C
LEVELS = 7
NH, NG = 8, 4
HEADS = NH + NG
PLE = 256
RANK = 16
EPS = 1e-6
SCALE = float(P) ** -0.5
TAU = 16.0
LN_MIN = 1e-19
D_H = D // 2

SLABS_H, SLABS_G = 4, 6
I_SLABS = NH * SLABS_H + NG * SLABS_G
E_SLABS, E_TILES = 2, KT
O_SLAB = I_SLABS + E_SLABS
G_SLAB = O_SLAB + KT
SLABS = G_SLAB + KT
E_TILE = I_SLABS
O_TILE = E_TILE + E_TILES
G_TILE = O_TILE + KT
TILES = G_TILE + KT
assert SLABS % 2 == 0 and TILES % 2 == 0
SIGS = 3 * HEADS + KT
SIGMOIDS = 3 * NH + 2 * NG + KT


def slab_columns():
    hq, hf, hi, hz = (i * D_H for i in range(4))
    gq = 4 * D_H
    gk = gq + NG * P
    gv = gk + NG * P
    gz = gv + D_H
    cols = []
    for n in range(NH):
        cols += [hi + n * P, hf + n * P, hq + n * P, hz + n * P]
    for m in range(NG):
        cols += [gv + 2 * m * P, gv + (2 * m + 1) * P, gk + m * P, gq + m * P,
                 gz + 2 * m * P, gz + (2 * m + 1) * P]
    return cols


class Steps:

    def __init__(self, eng, sem, spacer):
        self.eng, self.sem, self.n, self.spacer = eng, sem, 0, spacer

    def mark(self, ins):
        ins.then_inc(self.sem, 1)
        self.n += 1

    def wait(self):
        if self.n:
            self.eng.wait_ge(self.sem, self.n)

    def space(self):
        self.wait()
        self.mark(self.spacer())

    def fresh(self):
        self.space()
        if self.n:
            self.eng.wait_ge(self.sem, self.n)
            self.eng.sem_clear(self.sem)
            self.n = 0


def build(nc, x, p, slabs, w_glr, w2, vec, lb_rows, masks, restart, ident_d, out, e_scratch):
    with ExitStack() as ctx:
        def sb(name, shape, dt=F32):
            return ctx.enter_context(nc.sbuf_tensor(name, shape, dt))

        def sem(name):
            return ctx.enter_context(nc.semaphore(name))

        act_hi = sb("act_hi", [P, KT, TH], F32R)
        act_lo = sb("act_lo", [P, KT, TH], F32R)
        feat = sb("feat", [P, KT, TH])
        w_hi = [sb(f"w_hi{i}", [P, 2, 1024], F32R) for i in range(2)]
        w_lo = [sb(f"w_lo{i}", [P, 2, 1024], F32R) for i in range(2)]
        w_raw = [sb(f"w_raw{j}", [P, 1024]) for j in range(2)]
        work = sb("work", [P, 21, TH])

        def unit(i, n=1):
            v = work[:, i:i + n, :]
            return v.rearrange("p n t -> p (n t)")

        v_feat = unit(0, 2)
        q_t, k_t, b_t = unit(2), unit(3), unit(4)
        qb, kt = unit(5), unit(6)
        junk = unit(5, 2)
        kt_pos = unit(7)
        v_pos = unit(8, 2)
        on_pos = unit(10, 2)
        zs = unit(12, 2)
        s_in = unit(14, 2)
        attn = unit(16)
        t1, t2 = unit(17), unit(18)
        x_lv = [unit(19), unit(20)]
        mask_f32 = work[:, 17:21, :].rearrange("p n t -> p (n t)")[:, 0:LEVELS * TH // 2]
        x_in = work[:, 0:16, :].rearrange("p (t a) n -> p t (a n)", t=4)
        p_raw = unit(0, 2)
        e_buf = [unit(0), unit(1)]
        x_blk = [unit(0), unit(1)]
        xt_sb = [unit(2), unit(3)]
        h_sb = [unit(4), unit(5)]
        e_in = [unit(16), unit(19)]
        g_t, g_m = unit(20), unit(6)
        stage = [unit(17), unit(18), unit(19), unit(20)]

        sq_sum = sb("sq_sum", [P, TH])
        r_e = sb("r_e", [P, TH])
        glr_t = sb("glr_t", [P, TH])
        r_h = glr_t
        w2_sb = sb("w2_sb", [P, NG * P])
        w2_now = sb("w2_now", [P, P])
        restart_sb = sb("restart_sb", [P, TH])
        mask_sb = sb("mask_sb", [P, LEVELS, TH // 2], U8)
        ident = sb("ident", [P, P])
        ones = sb("ones", [P, P])
        glr_w = sb("glr_w", [P, KT, 2 * RANK], F32R)
        state_h = sb("state_h", [P, NH * P])
        state_g = sb("state_g", [P, NG * 2 * P])
        vecs = sb("vecs", [P, 32 + 3 * HEADS + 3 * KT])
        nmix = vecs[:, 0:16]
        pgn = vecs[:, 16:32]
        head_vec = vecs[:, 32:32 + 3 * HEADS]
        g_vec = vecs[:, 32 + 3 * HEADS:32 + 3 * HEADS + 3 * KT]
        lb_sb = sb("lb_sb", [P, 2, NH])
        lb_t = sb("lb_t", [P, 2, NH])
        hv_now = sb("hv_now", [P, 4])
        hv_rec = sb("hv_rec", [P, 4])
        gv_now = sb("gv_now", [P, 2, 4])
        small = sb("small", [P, 64])
        vec_dummy, act_dummy = sb("vec_dummy", [P, 1]), sb("act_dummy", [P, 1])
        x_ss, x_var, x_r, x_tmp = small[:, 0:16], small[:, 16:20], small[:, 20:24], small[:, 24:28]
        e_last, diag = small[:, 28:32], small[:, 32:36]
        o_ss, o_var, o_r, o_tmp = small[:, 36:40], small[:, 40:44], small[:, 44:48], small[:, 48:52]
        f_var, f_r, f_tmp = small[:, 52:56], small[:, 56:60], small[:, 60:64]

        def bank(name):
            return ctx.enter_context(nc.psum_tensor(name, [P, 512], F32))

        acc = [bank("acc0"), bank("acc1")]
        lv_ps = [bank("lv0"), bank("lv1")]
        so_ps = [bank("so0"), bank("so1")]
        tr_ps, ms_ps = bank("tr"), bank("ms")

        const_loaded, glrw_loaded = sem("const_loaded"), sem("glrw_loaded")
        const_ready = sem("const_ready")
        lb_arg, lb_exp = sem("lb_arg"), sem("lb_exp")
        x_loaded = [sem(f"x_loaded{i}") for i in range(4)]
        raw_loaded = [sem("raw_loaded0"), sem("raw_loaded1")]
        w_hi_ready, w_lo_ready = sem("w_hi_ready"), sem("w_lo_ready")
        act_hi_ready, act_lo_ready = sem("act_hi_ready"), sem("act_lo_ready")
        xt_ready = sem("xt_ready")
        xss_ready, xvar_ready, xy0_ready, xn_ready = (sem(s) for s in ("xss_ready", "xvar_ready", "xy0_ready", "xn_ready"))
        glr_ready, glrt_ready, glrw_hi = sem("glr_ready"), sem("glrt_ready"), sem("glrw_hi")
        glrw_ready, t1_zero = sem("glrw_ready"), sem("t1_zero")
        glrpos_ready, glrtr_ready = sem("glrpos_ready"), sem("glrtr_ready")
        h1_ready, g_arg = sem("h1_ready"), sem("g_arg")
        acc_ready = sem("acc_ready")
        acc_free = [sem("acc_free0"), sem("acc_free1")]
        sp_ready, ls_ready, sig_ready = sem("sp_ready"), sem("ls_ready"), sem("sig_ready")
        f_ready, g_ready = sem("f_ready"), sem("g_ready")
        logit_ready = sem("logit_ready")
        hv_ready = sem("hv_ready")
        vtr_ready, v_ready = sem("vtr_ready"), sem("v_ready")
        kt_arg, kt_exp, kt_ready = sem("kt_arg"), sem("kt_exp"), sem("kt_ready")
        qb_exp, qb_ready, elast_ready = sem("qb_exp"), sem("qb_ready"), sem("elast_ready")
        qk_ready, dgps_ready, dg_ready = sem("qk_ready"), sem("dgps_ready"), sem("dg_ready")
        kttr_ready, ktpos_ready = sem("kttr_ready"), sem("ktpos_ready")
        su_ready, s_ready = sem("su_ready"), sem("s_ready")
        lv_arg, lv_exp, lv_in = sem("lv_arg"), sem("lv_exp"), sem("lv_in")
        lv_ready, masked = sem("lv_ready"), sem("masked")
        o_ready, o_copied, oss_ready = sem("o_ready"), sem("o_copied"), sem("oss_ready")
        ovar_ready, oy0_ready, on_ready = sem("ovar_ready"), sem("oy0_ready"), sem("on_ready")
        ontr_ready, y_ready = sem("ontr_ready"), sem("y_ready")
        p_loaded, ptr_ready, pT_hi, pT_lo = sem("p_loaded"), sem("ptr_ready"), sem("pT_hi"), sem("pT_lo")
        e_sq, e_added = sem("e_sq"), sem("e_added")
        e_stored = [sem("e_stored0"), sem("e_stored1")]
        e_loaded = [sem("e_loaded0"), sem("e_loaded1")]
        e_used = sem("e_used")
        rows_ready, rvar_ready, ry0_ready = sem("rows_ready"), sem("rvar_ready"), sem("ry0_ready")
        xb_loaded = [sem("xb_loaded0"), sem("xb_loaded1")]
        xbt_ready, xt_copied = sem("xbt_ready"), sem("xt_copied")
        h_sq, h_added = sem("h_sq"), sem("h_added")
        g2_sq, g2_sum, g2_ready = sem("g2_sq"), sem("g2_sum"), sem("g2_ready")
        fsum_ready, fvar_ready, fy0_ready, fr_ready = (sem(s) for s in ("fsum_ready", "fvar_ready", "fy0_ready", "fr_ready"))
        ft_ready, ft_copied = sem("ft_ready"), sem("ft_copied")
        out_stored = [sem(f"out_stored{i}") for i in range(4)]
        act_steps, vec_steps = sem("act_steps"), sem("vec_steps")

        def tile_done(h, o):
            return h * TILES + (o + 3)

        def tile_free(h, half_no):
            return h * (TILES // 2) + (half_no + 2)

        block = ctx.enter_context(nc.Block())

        @block.sync
        def _(sp):
            for dst, src in ((vecs[:, :], vec), (lb_sb[:, :, :], lb_rows), (mask_f32, masks),
                             (restart_sb[:, :], restart), (ident[:, :], ident_d), (w2_sb[0:2 * RANK, :], w2)):
                sp.dma_start(dst, src).then_inc(const_loaded, 16)
            sp.dma_start(w_raw[0][:, 0:KT * RANK], w_glr).then_inc(glrw_loaded, 16)

            def load_slab(h, s, first=False):
                g = h * SLABS + s
                for j in range(2):
                    if not first:
                        sp.wait_ge(w_lo_ready, g * 2 + (j + 1))
                    sp.dma_start(w_raw[j][:, :], slabs[bass.ds(s, 1), j, :, :].rearrange("o p n -> (o p) n")
                                 ).then_inc(raw_loaded[j], 16)

            with sp.Fori(0, HALVES) as h:
                for t in range(4):
                    if t == 0:
                        for u in range(4):
                            sp.wait_ge(out_stored[u], h * 64 + 16)
                    sp.dma_start(x_in[:, t, :], x[h, t]).then_inc(x_loaded[t], 16)
                sp.wait_ge(glrw_ready, 1)
                with sp.Fori(0, I_SLABS + 1) as s:
                    load_slab(h, s)
                sp.wait_ge(vtr_ready, h * HEADS + HEADS)
                sp.dma_start(p_raw.rearrange("p (t n) -> p t n", t=4), p[h]).then_inc(p_loaded, 16)
                load_slab(h, I_SLABS + 1)

                def store_e(e):
                    sp.wait_ge(acc_free[e % 2], tile_free(h, (E_TILE + e) // 2))
                    sp.dma_start(e_scratch[e], e_buf[e % 2]).then_inc(e_stored[e % 2], 16)

                for e in range(8):
                    store_e(e)
                load_slab(h, O_SLAB)
                for e in range(8, E_TILES):
                    store_e(e)
                for u in range(2):
                    sp.wait_ge(e_stored[u], h * 128 + 128)

                def load_x_block(c, par, wait):
                    if wait:
                        sp.wait_ge(xbt_ready, h * KT + (c - 1))
                    sp.dma_start(x_blk[par].rearrange("p (t n) -> p t n", t=4),
                                 x[h].rearrange("t p d -> p t d")[:, :, bass.ds(c * P, P)]).then_inc(xb_loaded[par], 16)

                load_x_block(0, 0, False)
                load_x_block(1, 1, False)
                load_slab(h, O_SLAB + 1)
                load_slab(h, O_SLAB + 2)
                with sp.Fori(0, (KT - 2) // 2) as i:
                    for par in range(2):
                        load_x_block(i * 2 + (2 + par), par, True)
                        load_slab(h, i * 2 + (O_SLAB + 3 + par))
                sp.wait_ge(h_added, h * KT + KT)

                def load_e(c, par, wait):
                    if wait:
                        sp.wait_ge(e_used, h * KT + (c - 1))
                    sp.dma_start(e_in[par], e_scratch[bass.ds(c, 1), :, :].rearrange("o p n -> (o p) n")
                                 ).then_inc(e_loaded[par], 16)

                load_e(0, 0, False)
                load_e(1, 1, False)
                load_slab(h, G_SLAB + 1)
                with sp.Fori(0, (KT - 2) // 2) as i:
                    for par in range(2):
                        load_slab(h, i * 2 + (G_SLAB + 2 + par))
                        load_e(i * 2 + (2 + par), par, True)
                for n in range(16):
                    t, g = n // 4, n % 4
                    sp.wait_ge(ft_copied, h * 16 + (n + 1))
                    sp.dma_start(out[h, t][:, g * 512:(g + 1) * 512], stage[n % 4]).then_inc(out_stored[n % 4], 16)
            for u in range(4):
                sp.wait_ge(out_stored[u], HALVES * 64 + 16)

        @block.gpsimd
        def _(pool):
            for s, credit in ((out_stored[0], 16), (out_stored[1], 16), (out_stored[2], 16), (out_stored[3], 16),
                              (w_lo_ready, 2), (acc_ready, 2), (acc_free[0], 1), (acc_free[1], 1), (xt_copied, 2),
                              (ls_ready, 1), (o_copied, 1), (y_ready, 1), (masked, 2)):
                pool.sem_inc(s, credit)
            with pool.Fori(0, HALVES * SLABS // 2) as i:
                for par in range(2):
                    for j in range(2):
                        pool.wait_ge(w_hi_ready, i * 4 + (2 * par + j + 1))
                        nc.gpsimd.tensor_tensor(w_lo[par][:, j, :], w_raw[j][:, :],
                                                w_hi[par][:, j, :].bitcast(F32), ALU.subtract
                                                ).then_inc(w_lo_ready, 1)

        @block.tensor
        def _(pe):
            def passes(ps, lhs_hi, lhs_lo, rhs_hi, rhs_lo, start, stop):
                nc.tensor.matmul(ps, lhs_lo, rhs_hi, start=start, stop=False)
                nc.tensor.matmul(ps, lhs_hi, rhs_lo, start=False, stop=False)
                return nc.tensor.matmul(ps, lhs_hi, rhs_hi, start=False, stop=stop)

            def slab(h, s, o, par, half_no, hooks=None, act_from=None):
                hooks = hooks or {}
                pe.wait_ge(acc_free[par], h * (TILES // 2) + (half_no + 1))
                g = h * SLABS + s
                for k in range(KT):
                    if k % 8 == 0:
                        pe.wait_ge(w_hi_ready, g * 2 + (k // 8 + 1))
                        pe.wait_ge(w_lo_ready, g * 2 + (k // 8 + 3))
                    if act_from is not None:
                        pe.wait_ge(act_hi_ready, h * (3 * KT) + (act_from + k + 1))
                        pe.wait_ge(act_lo_ready, h * (3 * KT) + (act_from + k + 1))
                    cols = slice((k % 8) * P, (k % 8 + 1) * P)
                    last = passes(acc[par][:, :], w_hi[par][:, k // 8, cols], w_lo[par][:, k // 8, cols],
                                  act_hi[:, k, :], act_lo[:, k, :], k == 0, k == KT - 1)
                    if k == KT - 1:
                        last.then_inc(acc_ready, 1)
                    if k in hooks:
                        hooks[k]()

            def v_transpose(R, nb, h, half_no):
                pe.wait_ge(glrt_ready, h + 1)
                pe.wait_ge(acc_free[nb - 1], tile_free(h, half_no))
                pe.wait_ge(y_ready, R + 1)
                for vb in range(nb):
                    for c in range(NC_):
                        last = nc.tensor.transpose((tr_ps, ms_ps)[vb][:, c * P:(c + 1) * P],
                                                   v_feat[:, vb * TH + c * C:vb * TH + (c + 1) * C], ident[:, :])
                last.then_inc(vtr_ready, 1)

            def k_transpose(R):
                pe.wait_ge(kt_ready, R + 1)
                pe.wait_ge(v_ready, R + 1)
                for c in range(NC_):
                    last = nc.tensor.transpose(tr_ps[:, c * P:(c + 1) * P], kt[:, c * C:(c + 1) * C], ident[:, :])
                last.then_inc(kttr_ready, 1)
                pe.wait_ge(qk_ready, R + 1)
                for c in range(NC_):
                    last = nc.tensor.matmul(ms_ps[:, c:c + 1], x_lv[1][:, c * C:(c + 1) * C], ones[:, 0:1],
                                            start=True, stop=True)
                last.then_inc(dgps_ready, 1)

            def so_view(nb, c):
                return so_ps[(c * nb) // NC_][:, (c * nb) % NC_ * P:((c * nb) % NC_ + nb) * P]

            def state_update(R, nb):
                pe.wait_ge(ktpos_ready, R + 1)
                pe.wait_ge(o_copied, R + 1)
                for c in range(NC_):
                    last = nc.tensor.matmul(so_view(nb, c), kt_pos[:, c * P:(c + 1) * P],
                                            v_pos[:, c * nb * P:(c + 1) * nb * P], start=True, stop=True)
                last.then_inc(su_ready, 1)

            def level(R, l):
                pe.wait_ge(lv_in, R * LEVELS + (l + 1))
                pe.wait_ge(masked, R * LEVELS + (l + 1))
                s = 1 << l
                for c in range(NC_):
                    xc = x_lv[l % 2][:, c * C:(c + 1) * C]
                    upper = xc.rearrange("p (n two s) -> p n two s", two=2, s=s)[:, :, 1, :]
                    last = nc.tensor.matmul(lv_ps[l % 2][:, c * 64:(c + 1) * 64].rearrange("p (n s) -> p n s", s=s),
                                            xc, upper, start=True, stop=True)
                last.then_inc(lv_ready, 1)

            def readout(R, nb):
                pe.wait_ge(masked, R * LEVELS + (LEVELS + 2))
                pe.wait_ge(s_ready, R + 1)
                pe.wait_ge(qb_ready, R + 1)
                for c in range(NC_):
                    nc.tensor.matmul(so_view(nb, c), attn[:, c * C:(c + 1) * C],
                                     v_pos[:, c * nb * P:(c + 1) * nb * P], start=True, stop=False)
                    last = nc.tensor.matmul(so_view(nb, c), qb[:, c * C:(c + 1) * C],
                                            s_in[:, c * nb * P:(c + 1) * nb * P], start=False, stop=True)
                last.then_inc(o_ready, 1)

            def o_transpose(R, nb, logit_no=None):
                pe.wait_ge(on_ready, R + 1)
                if logit_no is not None:
                    pe.wait_ge(ls_ready, logit_no)
                for vb in range(nb):
                    for c in range(NC_):
                        last = nc.tensor.transpose((tr_ps, ms_ps)[vb][:, c * P:(c + 1) * P],
                                                   on_pos[:, (c * nb + vb) * P:(c * nb + vb + 1) * P], ident[:, :])
                last.then_inc(ontr_ready, 1)

            def gate_logits(R, m):
                pe.wait_ge(dg_ready, R)
                pe.wait_ge(hv_ready, R + 1)
                nc.tensor.matmul(ms_ps[:, :], w2_now[0:2 * RANK, :], glr_t[0:2 * RANK, :],
                                 start=True, stop=True).then_inc(logit_ready, 1)

            def levels(R, ls):
                return {k: (lambda l=l: level(R, l)) for k, l in ls}

            def hgrn_iteration(h, n, rec, first_hooks=None):
                r0 = h * HEADS + n
                hooks = [first_hooks or {}, {}, {}, {}]
                if rec:
                    R = r0 - 1
                    hooks[0] = {7: lambda: k_transpose(R), 15: lambda: state_update(R, 1)}
                    hooks[1] = levels(R, ((2, 0), (6, 1), (10, 2), (14, 3)))
                    hooks[2] = levels(R, ((2, 4), (6, 5), (10, 6)))
                    hooks[3] = {1: lambda: readout(R, 1), 11: lambda: o_transpose(R, 1)}
                hooks[3][15] = lambda: v_transpose(r0, 1, h, n * 2)
                for j in range(SLABS_H):
                    slab(h, n * SLABS_H + j, None, j % 2, n * 2 + j // 2, hooks[j],
                         0 if (not rec and j == 0) else None)

            def gla_iteration(h, m, rec_nb):
                r0 = h * HEADS + (m + NH)
                R = r0 - 1
                hooks = [{7: lambda: k_transpose(R), 15: lambda: state_update(R, rec_nb)},
                         levels(R, ((2, 0), (6, 1), (10, 2), (14, 3))),
                         levels(R, ((2, 4), (6, 5), (10, 6))),
                         {1: lambda: gate_logits(r0, m), 7: lambda: readout(R, rec_nb)},
                         {13: lambda: o_transpose(R, rec_nb, (h * SIGS + (m * 3 + (3 * NH + 2))))},
                         {11: lambda: v_transpose(r0, 2, h, m * 3 + NH * SLABS_H // 2)}]
                for j in range(SLABS_G):
                    slab(h, m * SLABS_G + (NH * SLABS_H + j), None, j % 2,
                         m * 3 + (NH * SLABS_H // 2 + j // 2), hooks[j])

            pe.wait_ge(const_loaded, 16 * 6)
            pe.wait_ge(const_ready, 1)
            with pe.Fori(0, HALVES) as h:
                ring = [lv_ps[0], lv_ps[1], so_ps[0], so_ps[1], tr_ps]
                pe.wait_ge(xn_ready, h * 4 + 4)
                for k in range(KT):
                    if k >= len(ring):
                        pe.wait_ge(act_lo_ready, h * (3 * KT) + (k - len(ring) + 1))
                        pe.wait_ge(act_hi_ready, h * (3 * KT) + (k - len(ring) + 1))
                    for t in range(4):
                        last = nc.tensor.transpose(ring[k % len(ring)][:, t * P:(t + 1) * P],
                                                   x_in[:, t, k * P:(k + 1) * P], ident[:, :])
                    last.then_inc(xt_ready, 1)
                pe.wait_ge(glrw_ready, 1)
                for t in range(4):
                    for k in range(KT):
                        if t == 0:
                            pe.wait_ge(act_hi_ready, h * (3 * KT) + (k + 1))
                            pe.wait_ge(act_lo_ready, h * (3 * KT) + (k + 1))
                        cols = slice(t * 2 * RANK, (t + 1) * 2 * RANK)
                        nc.tensor.matmul(ms_ps[:, cols], act_lo[:, k, t * P:(t + 1) * P], glr_w[:, k, :],
                                         start=(k == 0), stop=False)
                        last = nc.tensor.matmul(ms_ps[:, cols], act_hi[:, k, t * P:(t + 1) * P], glr_w[:, k, :],
                                                start=False, stop=(k == KT - 1))
                last.then_inc(glr_ready, 1)
                def glr_transpose():
                    pe.wait_ge(glrpos_ready, h + 1)
                    for t in range(4):
                        last = nc.tensor.transpose(tr_ps[:, t * P:(t + 1) * P], t1[:, t * P:(t + 1) * P], ident[:, :])
                    last.then_inc(glrtr_ready, 1)

                hgrn_iteration(h, 0, False, {3: glr_transpose})
                with pe.Fori(1, NH) as n:
                    hgrn_iteration(h, n, True)
                gla_iteration(h, 0, 1)
                with pe.Fori(1, NG) as m:
                    gla_iteration(h, m, 2)
                R = h * HEADS + (HEADS - 1)
                k_transpose(R)
                pe.wait_ge(p_loaded, h * 16 + 16)
                pe.wait_ge(ktpos_ready, R + 1)
                pe.wait_ge(dg_ready, R + 1)
                for k in range(2):
                    for t in range(4):
                        last = nc.tensor.transpose((tr_ps, ms_ps)[k][:, t * P:(t + 1) * P],
                                                   p_raw[:, t * PLE + k * P:t * PLE + (k + 1) * P], ident[:, :])
                    last.then_inc(ptr_ready, 1)
                state_update(R, 2)
                pe.wait_ge(pT_hi, h * 2 + 2)
                pe.wait_ge(pT_lo, h * 2 + 2)
                hooks = {e: (lambda l=l: level(R, l)) for e, l in ((0, 0), (1, 1), (3, 2), (4, 3), (6, 4), (8, 5), (9, 6))}
                hooks[11] = lambda: readout(R, 2)
                for e in range(E_TILES):
                    s, par, o = I_SLABS + e // 8, e % 2, E_TILE + e
                    if e % 8 == 0:
                        pe.wait_ge(w_hi_ready, (h * SLABS + s) * 2 + 2)
                        pe.wait_ge(w_lo_ready, (h * SLABS + s) * 2 + 4)
                    pe.wait_ge(acc_free[par], h * (TILES // 2) + (o // 2 + 1))
                    cols = slice((e % 8) * P, (e % 8 + 1) * P)
                    for k in range(2):
                        last = passes(acc[par][:, :], w_hi[s % 2][:, k, cols], w_lo[s % 2][:, k, cols],
                                      act_hi[:, KT - 2 + k, :], act_lo[:, KT - 2 + k, :], k == 0, k == 1)
                    last.then_inc(acc_ready, 1)
                    if e in hooks:
                        hooks[e]()
                o_transpose(R, 2)
                pe.wait_ge(y_ready, h * HEADS + (HEADS + 1))
                pe.wait_ge(e_added, h * E_TILES + E_TILES)
                nc.tensor.matmul(ms_ps[:, :], ones[:, :], sq_sum[:, :], start=True, stop=True).then_inc(rows_ready, 1)

                def o_pair(i, first):
                    for par in range(2):
                        c = i * 2 + par

                        def x_transpose():
                            pe.wait_ge(xb_loaded[par], (h * 8 + i) * 16 + 16)
                            pe.wait_ge(xt_copied, h * KT + (c + 1))
                            if first and par == 1:
                                pe.wait_ge(rvar_ready, h * 2 + 1)
                            for t in range(4):
                                last = nc.tensor.transpose((tr_ps, ms_ps)[par][:, t * P:(t + 1) * P],
                                                           x_blk[par][:, t * P:(t + 1) * P], ident[:, :])
                            last.then_inc(xbt_ready, 1)

                        slab(h, c + O_SLAB, None, par, i + O_TILE // 2, {9: x_transpose},
                             KT if (first and par == 0) else None)

                o_pair(0, True)
                with pe.Fori(1, KT // 2) as i:
                    o_pair(i, False)
                def g_pair(i, first):
                    for par in range(2):
                        hooks = {}
                        if first and par == 0:
                            def h_rows():
                                pe.wait_ge(h_added, h * KT + KT)
                                pe.wait_ge(xt_copied, h * KT + (KT + 2))
                                nc.tensor.matmul(ms_ps[:, :], ones[:, :], sq_sum[:, :], start=True,
                                                 stop=True).then_inc(rows_ready, 1)
                            hooks = {11: h_rows}
                        slab(h, i * 2 + (G_SLAB + par), None, par, i + G_TILE // 2, hooks,
                             2 * KT if (first and par == 0) else None)

                g_pair(0, True)
                with pe.Fori(1, KT // 2) as i:
                    g_pair(i, False)
                pe.wait_ge(g2_ready, h * KT + KT)
                for t in range(4):
                    last = nc.tensor.matmul(ms_ps[:, t:t + 1], sq_sum[:, t * P:(t + 1) * P], ones[:, 0:1],
                                            start=True, stop=True)
                last.then_inc(fsum_ready, 1)
                banks = [lv_ps[0], lv_ps[1], so_ps[0], so_ps[1]]
                for n in range(16):
                    t, g = n // 4, n % 4
                    if n >= 4:
                        pe.wait_ge(ft_copied, h * 16 + (n - 3))
                    for j in range(4):
                        last = nc.tensor.transpose(banks[n % 4][:, j * P:(j + 1) * P],
                                                   feat[:, 4 * g + j, t * P:(t + 1) * P], ident[:, :])
                    last.then_inc(ft_ready, 1)
                pe.wait_ge(ft_copied, h * 16 + 16)

        @block.scalar
        def _(act):
            st = Steps(act, act_steps, lambda: nc.scalar.copy(act_dummy[:, :], vecs[:, 0:1]))
            A = nc.scalar.activation
            act.preload_act_table_set("natural_log_exp_and_others")

            def split_weights(h, s, par, prev_tile):
                act.wait_ge(acc_ready, h * TILES + (prev_tile + 3))
                g = h * SLABS + s
                for j in range(2):
                    act.wait_ge(raw_loaded[j], g * 16 + 16)
                    nc.scalar.copy(w_hi[par][:, j, :], w_raw[j][:, :]).then_inc(w_hi_ready, 1)

            def softplus(h, no, src, ready_sem, ready_val, bias=None):
                act.wait_ge(ready_sem, ready_val)
                act.wait_ge(ls_ready, h * SIGS + (no + 1))
                st.mark(A(t1, src, ACT.Abs) if bias is None else A(t1, src, ACT.Abs, bias=bias))
                st.wait()
                st.mark(A(t1, t1, ACT.Exp, scale=-1.0))
                st.wait()
                A(t1, t1, ACT.Ln, bias=1.0).then_inc(sp_ready, 1)

            def sigmoid(h, no):
                act.wait_ge(ls_ready, h * SIGS + (no + 2))
                A(t2, t2, ACT.Exp).then_inc(sig_ready, 1)

            def rec_decays(R):
                act.wait_ge(kt_arg, R + 1)
                A(kt, kt, ACT.Exp).then_inc(kt_exp, 1)
                A(qb, b_t, ACT.Exp).then_inc(qb_exp, 1)
                A(e_last, b_t[:, C - 1:TH:C], ACT.Exp).then_inc(elast_ready, 1)

            def rec_level(R, l):
                act.wait_ge(lv_arg, R * LEVELS + (l + 1))
                A(x_lv[l % 2], x_lv[l % 2], ACT.Exp).then_inc(lv_exp, 1)

            def k_copy(R):
                act.wait_ge(kttr_ready, R + 1)
                nc.scalar.copy(kt_pos, tr_ps[:, :]).then_inc(ktpos_ready, 1)
                act.wait_ge(dgps_ready, R + 1)
                nc.scalar.copy(diag, ms_ps[:, 0:NC_]).then_inc(dg_ready, 1)

            def v_copy_feat(h, o, par, vb):
                act.wait_ge(acc_ready, tile_done(h, o))
                A(v_feat[:, vb * TH:(vb + 1) * TH], acc[par][:, :], ACT.Copy).then_inc(acc_free[par], 1)

            def v_copy(R, nb):
                act.wait_ge(vtr_ready, R + 1)
                v = v_pos[:, 0:NC_ * nb * P].rearrange("p (c b n) -> p c b n", b=nb, n=P)
                for vb in range(nb):
                    ins = nc.scalar.copy(v[:, :, vb, :], (tr_ps, ms_ps)[vb][:, :].rearrange("p (c n) -> p c n", n=P))
                    ins.then_inc(v_ready, 1) if vb == nb - 1 else st.mark(ins)

            def o_squares(R, nb):
                act.wait_ge(o_copied, R + 2)
                for c in range(NC_):
                    ins = A(junk[:, c * nb * P:(c + 1) * nb * P], on_pos[:, c * nb * P:(c + 1) * nb * P],
                            ACT.Square, accum_out=o_ss[:, c:c + 1])
                    ins.then_inc(oss_ready, 1) if c == NC_ - 1 else st.mark(ins)
                act.wait_ge(ovar_ready, R + 1)
                st.mark(A(o_tmp, o_var, ACT.Ln))
                st.wait()
                A(o_r, o_tmp, ACT.Exp, scale=-0.5).then_inc(oy0_ready, 1)

            def hgrn_iteration(h, n, rec):
                r0 = h * HEADS + n
                R = r0 - 1
                s = n * SLABS_H
                sg = n * 3
                if rec:
                    rec_decays(R)
                    split_weights(h, s + 1, 1, s - 1)
                    rec_level(R, 0)
                    softplus(h, sg - 1, acc[1][:, :], acc_ready, tile_done(h, s - 1))
                    sigmoid(h, sg - 1)
                    k_copy(R)
                    rec_level(R, 1)
                split_weights(h, s + 2, 0, s)
                v_copy_feat(h, s, 0, 0)
                if rec:
                    for l in (2, 3):
                        rec_level(R, l)
                    for l in (4, 5):
                        rec_level(R, l)
                split_weights(h, s + 3, 1, s + 1)
                if rec:
                    rec_level(R, 6)
                softplus(h, sg, acc[1][:, :], acc_ready, tile_done(h, s + 1))
                sigmoid(h, sg)
                act.wait_ge(f_ready, h * NH + (n + 1))
                A(t2, t2, ACT.Ln).then_inc(g_ready, 1)
                split_weights(h, s + 4, 0, s + 2)
                if rec:
                    o_squares(R, 1)
                softplus(h, sg + 1, acc[0][:, :], acc_ready, tile_done(h, s + 2))
                sigmoid(h, sg + 1)
                v_copy(r0, 1)

            def gla_iteration(h, m, rec_nb):
                r0 = h * HEADS + (m + NH)
                R = r0 - 1
                s = m * SLABS_G + NH * SLABS_H
                sg = m * 3 + 3 * NH
                rec_decays(R)
                split_weights(h, s + 1, 1, s - 1)
                rec_level(R, 0)
                softplus(h, sg - 1, acc[1][:, :], acc_ready, tile_done(h, s - 1))
                sigmoid(h, sg - 1)
                k_copy(R)
                rec_level(R, 1)
                split_weights(h, s + 2, 0, s)
                v_copy_feat(h, s, 0, 0)
                for l in (2, 3, 4):
                    rec_level(R, l)
                split_weights(h, s + 3, 1, s + 1)
                rec_level(R, 5)
                v_copy_feat(h, s + 1, 1, 1)
                rec_level(R, 6)
                split_weights(h, s + 4, 0, s + 2)
                act.wait_ge(hv_ready, r0 + 1)
                softplus(h, sg, ms_ps[:, :], logit_ready, h * NG + (m + 1), bias=hv_now[:, 0:1])
                split_weights(h, s + 5, 1, s + 3)
                o_squares(R, rec_nb)
                split_weights(h, s + 6, 0, s + 4)
                softplus(h, sg + 1, acc[0][:, :], acc_ready, tile_done(h, s + 4))
                sigmoid(h, sg + 1)
                v_copy(r0, 2)

            act.wait_ge(const_loaded, 16 * 6)
            act.wait_ge(glrw_loaded, 16)
            nc.scalar.copy(glr_w[:, :, 0:RANK], w_raw[0][:, 0:KT * RANK].rearrange("p (k n) -> p k n", n=RANK)
                           ).then_inc(glrw_hi, 1)
            act.wait_ge(lb_arg, 1)
            A(lb_t[:, :, :], lb_t[:, :, :], ACT.Exp).then_inc(lb_exp, 1)
            st.fresh()
            with act.Fori(0, HALVES) as h:
                for t in range(4):
                    act.wait_ge(x_loaded[t], h * 16 + 16)
                    for a in range(4):
                        if a or t:
                            st.wait()
                        ins = A(ms_ps[:, :], x_in[:, t, a * 512:(a + 1) * 512], ACT.Square,
                                accum_out=x_ss[:, t * 4 + a:t * 4 + a + 1])
                        ins.then_inc(xss_ready, 1) if (t, a) == (3, 3) else st.mark(ins)
                act.wait_ge(xvar_ready, h + 1)
                st.mark(A(x_tmp, x_var, ACT.Ln))
                st.wait()
                A(x_r, x_tmp, ACT.Exp, scale=-0.5).then_inc(xy0_ready, 1)
                ring = [lv_ps[0], lv_ps[1], so_ps[0], so_ps[1], tr_ps]
                split_weights(h, 0, 0, -2)
                act.wait_ge(acc_ready, h * TILES + 2)
                for k in range(KT):
                    act.wait_ge(xt_ready, h * KT + (k + 1))
                    A(act_hi[:, k, :], ring[k % 5][:, :], ACT.Copy, scale=nmix[:, k:k + 1]).then_inc(act_hi_ready, 1)
                act.wait_ge(glr_ready, h + 1)
                act.wait_ge(t1_zero, h + 1)
                nc.scalar.copy(t1.rearrange("p (t n) -> p t n", t=4)[:, :, 0:2 * RANK],
                               ms_ps[:, 0:8 * RANK].rearrange("p (t n) -> p t n", t=4)).then_inc(glrpos_ready, 1)
                split_weights(h, 1, 1, -1)
                act.wait_ge(glrtr_ready, h + 1)
                nc.scalar.copy(glr_t[0:2 * RANK, :], tr_ps[0:2 * RANK, :]).then_inc(glrt_ready, 1)
                hgrn_iteration(h, 0, False)
                st.fresh()
                with act.Fori(1, NH) as n:
                    hgrn_iteration(h, n, True)
                    st.fresh()
                gla_iteration(h, 0, 1)
                st.fresh()
                with act.Fori(1, NG) as m:
                    gla_iteration(h, m, 2)
                    st.fresh()
                R = h * HEADS + (HEADS - 1)
                sg = 3 * HEADS - 1
                rec_decays(R)
                split_weights(h, I_SLABS + 1, 1, I_SLABS - 1)
                rec_level(R, 0)
                softplus(h, sg, acc[1][:, :], acc_ready, tile_done(h, I_SLABS - 1))
                sigmoid(h, sg)
                k_copy(R)
                rec_level(R, 1)
                for k in range(2):
                    act.wait_ge(ptr_ready, h * 2 + (k + 1))
                    nc.scalar.copy(act_hi[:, KT - 2 + k, :], (tr_ps, ms_ps)[k][:, :]).then_inc(pT_hi, 1)
                after = {0: 2, 1: 3, 3: 4, 4: 5, 6: 6}
                for e in range(E_TILES):
                    par = e % 2
                    if e == 8:
                        split_weights(h, O_SLAB, 0, E_TILE + 7)
                    act.wait_ge(acc_ready, tile_done(h, E_TILE + e))
                    if e >= 2:
                        act.wait_ge(e_stored[par], h * 128 + 16 * (e // 2))
                        act.wait_ge(e_added, h * E_TILES + (e - 1))
                    elif e == 0:
                        act.wait_ge(acc_free[1], tile_free(h, (I_SLABS - 1) // 2))
                    A((t1, t2)[par], acc[par][:, :], ACT.Square).then_inc(e_sq, 1)
                    nc.scalar.copy(e_buf[par], acc[par][:, :]).then_inc(acc_free[par], 1)
                    if e in after:
                        rec_level(R, after[e])
                    if e == 13:
                        o_squares(R, 2)
                st.fresh()
                for k in range(KT):
                    if k == 0:
                        act.wait_ge(y_ready, h * HEADS + HEADS)
                    if k == KT - 2:
                        act.wait_ge(y_ready, h * HEADS + (HEADS + 1))
                        act.wait_ge(acc_ready, tile_done(h, O_TILE - 1))
                    nc.scalar.copy(act_hi[:, k, :], feat[:, k, :]).then_inc(act_hi_ready, 1)

                rv = h * 2 + 1
                act.wait_ge(rvar_ready, rv)
                st.mark(A(t2, t1, ACT.Ln))
                st.wait()
                A(t2, t2, ACT.Exp, scale=-0.5).then_inc(ry0_ready, 1)
                st.fresh()

                def o_pair(i):
                    for par in range(2):
                        c = i * 2 + par
                        split_weights(h, c + (O_SLAB + 1), 1 - par, c + (O_TILE - 1))
                        act.wait_ge(xbt_ready, h * KT + (c + 1))
                        nc.scalar.copy(xt_sb[par], (tr_ps, ms_ps)[par][:, :]).then_inc(xt_copied, 1)
                        act.wait_ge(acc_free[par], tile_free(h, i + O_TILE // 2))
                        A((t1, t2)[par], h_sb[par], ACT.Square).then_inc(h_sq, 1)

                with act.Fori(0, KT // 2) as i:
                    o_pair(i)
                for k in range(KT):
                    if k == 0:
                        act.wait_ge(h1_ready, h * KT + KT)
                        act.wait_ge(acc_ready, tile_done(h, G_TILE - 1))
                    A(act_hi[:, k, :], feat[:, k, :], ACT.Copy, scale=pgn[:, k:k + 1]).then_inc(act_hi_ready, 1)
                act.wait_ge(rvar_ready, rv + 1)
                st.mark(A(t2, t1, ACT.Ln))
                st.wait()
                A(t2, t2, ACT.Exp, scale=-0.5).then_inc(ry0_ready, 1)
                st.fresh()

                def g_split(i, par):
                    split_weights(h, i * 2 + (G_SLAB + 1 + par), 1 - par, i * 2 + (G_TILE - 1 + par))

                def g_gate(i, par):
                    no = i * 2 + (3 * HEADS + par)
                    softplus(h, no, g_t, g_arg, h * KT + (i * 2 + par + 1))
                    sigmoid(h, no)
                    act.wait_ge(g2_sum, h * KT + (i * 2 + par + 1))
                    A(t1, g_t, ACT.Square).then_inc(g2_sq, 1)

                with act.Fori(0, KT // 2 - 1) as i:
                    for par in range(2):
                        g_split(i, par)
                        g_gate(i, par)
                    st.fresh()
                g_split(KT // 2 - 1, 0)
                g_gate(KT // 2 - 1, 0)
                g_gate(KT // 2 - 1, 1)
                act.wait_ge(fvar_ready, h + 1)
                st.mark(A(f_tmp, f_var, ACT.Ln))
                st.wait()
                A(f_r, f_tmp, ACT.Exp, scale=-0.5).then_inc(fy0_ready, 1)
                st.fresh()

        @block.vector
        def _(vec_e):
            v = nc.vector
            st = Steps(vec_e, vec_steps, lambda: v.memset(vec_dummy[:, :], 0.0))

            def newton(r, y0, var, tmp):
                st.mark(v.tensor_tensor(tmp, y0, y0, ALU.mult))
                st.wait()
                st.mark(v.tensor_tensor(tmp, tmp, var, ALU.mult))
                st.wait()
                st.mark(v.tensor_scalar(tmp, tmp, -0.5, 1.5, ALU.mult, ALU.add))
                st.wait()
                return v.tensor_tensor(r, y0, tmp, ALU.mult)

            def log_sigmoid(h, no, src):
                vec_e.wait_ge(sp_ready, h * SIGS + (no + 1))
                st.wait()
                v.scalar_tensor_tensor(out=t2, in0=src, scalar=0.0, in1=t1, op0=ALU.min, op1=ALU.subtract
                                       ).then_inc(ls_ready, 1)

            def silu(h, sig_no, dst, src, scale, par):
                vec_e.wait_ge(sig_ready, h * SIGMOIDS + (sig_no + 1))
                v.scalar_tensor_tensor(out=dst, in0=src, scalar=scale, in1=t2, op0=ALU.mult, op1=ALU.mult
                                       ).then_inc(acc_free[par], 1)

            def rec_begin(R):
                b3 = b_t.rearrange("p (c n) -> p c n", n=C)
                st.wait()
                v.tensor_tensor(kt.rearrange("p (c n) -> p c n", n=C), b3[:, :, C - 1:C].to_broadcast([P, NC_, C]),
                                b3, ALU.subtract).then_inc(kt_arg, 1)
                v.tensor_tensor(x_lv[1], q_t, k_t, ALU.mult).then_inc(qk_ready, 1)

            def halves_of(t, l):
                b4 = t.rearrange("p (n two s) -> p n two s", two=2, s=1 << l)
                return b4[:, :, 0, :], b4[:, :, 1, :]

            def level_arg(R, l):
                s = 1 << l
                blo, bup = halves_of(b_t, l)
                xlo, xup = halves_of(x_lv[l % 2], l)
                mid = blo[:, :, s - 1:s].to_broadcast([P, TH // (2 * s), s])
                st.mark(v.tensor_tensor(xlo, mid, blo, ALU.subtract))
                v.tensor_tensor(xup, bup, mid, ALU.subtract).then_inc(lv_arg, 1)

            def level_mul(R, l):
                vec_e.wait_ge(lv_exp, R * LEVELS + (l + 1))
                xlo, xup = halves_of(x_lv[l % 2], l)
                klo, _ = halves_of(k_t, l)
                _, qup = halves_of(q_t, l)
                st.mark(v.tensor_tensor(xlo, xlo, klo, ALU.mult))
                v.tensor_tensor(xup, xup, qup, ALU.mult).then_inc(lv_in, 1)

            def mask_level(R, l):
                vec_e.wait_ge(lv_ready, R * LEVELS + (l + 1))
                s = 1 << l
                st.space()
                st.wait()
                v.copy_predicated(halves_of(attn, l)[1], mask_sb[:, l, :].rearrange("p (n s) -> p n s", s=s),
                                  lv_ps[l % 2][:, 0:TH // 2].rearrange("p (n s) -> p n s", s=s)
                                  ).then_inc(masked, 1)

            def decayed(R):
                vec_e.wait_ge(kt_exp, R + 1)
                v.tensor_tensor(kt, kt, k_t, ALU.mult).then_inc(kt_ready, 1)
                vec_e.wait_ge(qb_exp, R + 1)
                v.tensor_tensor(qb, qb, q_t, ALU.mult).then_inc(qb_ready, 1)

            def state_chain(R, nb, state):
                w = nb * P
                st.mark(v.tensor_copy(s_in[:, 0:w], state))
                vec_e.wait_ge(su_ready, R + 1)
                vec_e.wait_ge(elast_ready, R + 1)
                for c in range(NC_):
                    st.wait()
                    dst = s_in[:, (c + 1) * w:(c + 2) * w] if c < NC_ - 1 else state
                    ps = so_ps[(c * nb) // NC_][:, (c * nb) % NC_ * P:((c * nb) % NC_ + nb) * P]
                    ins = v.scalar_tensor_tensor(out=dst, in0=s_in[:, c * w:(c + 1) * w], scalar=e_last[:, c:c + 1],
                                                 in1=ps, op0=ALU.mult, op1=ALU.add)
                    st.mark(ins) if c < NC_ - 1 else ins.then_inc(s_ready, 1)

            def o_copy(R, nb):
                w = nb * P
                vec_e.wait_ge(o_ready, R + 1)
                vec_e.wait_ge(dg_ready, R + 1)
                for c in range(NC_):
                    ps = so_ps[(c * nb) // NC_][:, (c * nb) % NC_ * P:((c * nb) % NC_ + nb) * P]
                    ins = v.scalar_tensor_tensor(out=on_pos[:, c * w:(c + 1) * w], in0=v_pos[:, c * w:(c + 1) * w],
                                                 scalar=diag[:, c:c + 1], in1=ps, op0=ALU.mult, op1=ALU.add)
                    st.mark(ins) if c < NC_ - 1 else ins.then_inc(o_copied, 1)

            def o_norm(R, nb):
                w = nb * P
                vec_e.wait_ge(oss_ready, R + 1)
                v.tensor_scalar(o_var, o_ss, 1.0 / w, EPS, ALU.mult, ALU.add).then_inc(ovar_ready, 1)
                vec_e.wait_ge(oy0_ready, R + 1)
                st.mark(newton(o_r, o_r, o_var, o_tmp))
                st.wait()
                for c in range(NC_):
                    ins = v.tensor_scalar(on_pos[:, c * w:(c + 1) * w], on_pos[:, c * w:(c + 1) * w],
                                          o_r[:, c:c + 1], None, ALU.mult)
                    st.mark(ins) if c < NC_ - 1 else ins.then_inc(on_ready, 1)

            def y_out(R, nb, k0, norm_col):
                vec_e.wait_ge(ontr_ready, R + 1)
                for vb in range(nb):
                    dst = feat[:, bass.ds(k0 + vb, 1), :].rearrange("p o n -> p (o n)")
                    ins = v.scalar_tensor_tensor(out=dst, in0=(tr_ps, ms_ps)[vb][:, :],
                                                 scalar=hv_rec[:, norm_col + vb:norm_col + vb + 1],
                                                 in1=zs[:, vb * TH:(vb + 1) * TH], op0=ALU.mult, op1=ALU.mult)
                    st.mark(ins) if vb < nb - 1 else ins.then_inc(y_ready, 1)

            def head_constants(r0, r, w2_m=None):
                st.wait()
                st.mark(v.tensor_copy(hv_rec[:, 0:3], hv_now[:, 0:3]))
                st.wait()
                if w2_m is not None:
                    st.mark(v.tensor_copy(w2_now[0:2 * RANK, :], w2_sb[0:2 * RANK, bass.ds(w2_m * P, P)]))
                v.tensor_copy(hv_now[:, 0:3], head_vec[:, bass.ds(r * 3, 3)]).then_inc(hv_ready, 1)

            def rec_first(h, R, z_no, z_sig, z_dst):
                decayed(R)
                level_arg(R, 0)
                level_mul(R, 0)
                log_sigmoid(h, z_no, acc[1][:, :])
                silu(h, z_sig, z_dst, acc[1][:, :], 1.0, 1)
                vec_e.wait_ge(dgps_ready, R + 1)
                level_arg(R, 1)
                level_mul(R, 1)

            def next_level(R, l):
                mask_level(R, l)
                level_arg(R, l + 2)
                level_mul(R, l + 2)

            def hgrn_iteration(h, n, rec):
                r0 = h * HEADS + n
                R = r0 - 1
                s, sg = n * SLABS_H, n * 3
                head_constants(r0, n)
                if rec:
                    rec_first(h, R, sg - 1, sg - 1, zs[:, 0:TH])
                    state_chain(R, 1, state_h[:, bass.ds((n - 1) * P, P)])
                    for l in range(LEVELS - 2):
                        next_level(R, l)
                vec_e.wait_ge(hv_ready, r0 + 1)
                log_sigmoid(h, sg, acc[1][:, :])
                vec_e.wait_ge(sig_ready, h * SIGMOIDS + (sg + 1))
                v.tensor_scalar(t2, t2, hv_now[:, 1:2], hv_now[:, 0:1], ALU.mult, ALU.add).then_inc(acc_free[1], 1)
                vec_e.wait_ge(acc_free[1], tile_free(h, n * 2))
                st.mark(v.tensor_scalar(k_t, t2, -1.0, 1.0, ALU.mult, ALU.add))
                st.wait()
                v.tensor_scalar(t2, t2, LN_MIN, None, ALU.max).then_inc(f_ready, 1)
                if rec:
                    mask_level(R, LEVELS - 2)
                vec_e.wait_ge(g_ready, h * NH + (n + 1))
                st.mark(v.tensor_tensor_scan(b_t, restart_sb[:, :], t2, 0.0, ALU.mult, ALU.add))
                if rec:
                    mask_level(R, LEVELS - 1)
                    o_copy(R, 1)
                    o_norm(R, 1)
                log_sigmoid(h, sg + 1, acc[0][:, :])
                silu(h, sg + 1, q_t, acc[0][:, :], SCALE, 0)
                vec_e.wait_ge(acc_free[0], tile_free(h, n * 2 + 1))
                if rec:
                    y_out(R, 1, n - 1, 2)
                rec_begin(r0)

            def gla_iteration(h, m, rec_nb):
                r0 = h * HEADS + (m + NH)
                R = r0 - 1
                half = NH * SLABS_H // 2 + m * 3 if isinstance(m, int) else m * 3 + NH * SLABS_H // 2
                s, sg, sig = m * SLABS_G + NH * SLABS_H, m * 3 + 3 * NH, m * 2 + 3 * NH
                head_constants(r0, m + NH, m)
                zb = rec_nb - 1
                rec_first(h, R, sg - 1, sig - 1, zs[:, zb * TH:(zb + 1) * TH])
                state_chain(R, rec_nb, state_h[:, (NH - 1) * P:NH * P] if rec_nb == 1
                            else state_g[:, bass.ds((m - 1) * 2 * P, 2 * P)])
                for l in range(LEVELS - 2):
                    next_level(R, l)
                vec_e.wait_ge(lv_in, R * LEVELS + LEVELS)
                vec_e.wait_ge(acc_ready, tile_done(h, s + 2))
                v.tensor_copy(k_t, acc[0][:, :]).then_inc(acc_free[0], 1)
                for l in (LEVELS - 2, LEVELS - 1):
                    mask_level(R, l)
                vec_e.wait_ge(hv_ready, r0 + 1)
                vec_e.wait_ge(sp_ready, h * SIGS + (sg + 1))
                st.mark(v.tensor_scalar(t2, ms_ps[:, :], hv_now[:, 0:1], 0.0, ALU.add, ALU.min))
                st.wait()
                v.tensor_tensor(t2, t2, t1, ALU.subtract).then_inc(ls_ready, 1)
                vec_e.wait_ge(ls_ready, h * SIGS + (sg + 2))
                st.mark(v.tensor_tensor_scan(b_t, restart_sb[:, :], t2, 0.0, ALU.mult, ALU.add))
                st.wait()
                st.mark(v.tensor_scalar(b_t, b_t, 1.0 / TAU, None, ALU.mult))
                vec_e.wait_ge(acc_ready, tile_done(h, s + 3))
                v.tensor_scalar(q_t, acc[1][:, :], SCALE, None, ALU.mult).then_inc(acc_free[1], 1)
                o_copy(R, rec_nb)
                o_norm(R, rec_nb)
                y_out(R, rec_nb, NH - 1 if rec_nb == 1 else (m - 1) * 2 + NH, 2 if rec_nb == 1 else 1)
                log_sigmoid(h, sg + 1, acc[0][:, :])
                vec_e.wait_ge(y_ready, R + 2)
                silu(h, sig, zs[:, 0:TH], acc[0][:, :], 1.0, 0)
                vec_e.wait_ge(acc_free[0], tile_free(h, half + 2))
                rec_begin(r0)

            st.mark(v.memset(state_h[:, :], 0.0))
            st.mark(v.memset(state_g[:, :], 0.0))
            v.memset(ones[:, :], 1.0).then_inc(const_ready, 1)
            vec_e.wait_ge(glrw_hi, 1)
            v.tensor_tensor(glr_w[:, :, RANK:2 * RANK], w_raw[0][:, 0:KT * RANK].rearrange("p (k n) -> p k n", n=RANK),
                            glr_w[:, :, 0:RANK].bitcast(F32), ALU.subtract).then_inc(glrw_ready, 1)
            vec_e.wait_ge(const_loaded, 16 * 6)
            st.mark(v.tensor_copy(mask_sb[:, :, :],
                                  mask_f32.rearrange("p (l n) -> p l n", l=LEVELS)))
            st.mark(v.tensor_tensor(lb_t[:, 0, :], lb_sb[:, 0, :], lb_sb[:, 1, :], ALU.max))
            st.wait()
            st.mark(v.tensor_tensor(lb_t[:, 1, :], lb_sb[:, 1, :], lb_t[:, 0, :], ALU.subtract))
            st.wait()
            v.tensor_tensor(lb_t[:, 0, :], lb_sb[:, 0, :], lb_t[:, 0, :], ALU.subtract).then_inc(lb_arg, 1)
            vec_e.wait_ge(lb_exp, 1)
            st.mark(v.tensor_tensor(lb_sb[:, 0, :], lb_t[:, 0, :], lb_t[:, 1, :], ALU.add))
            st.wait()
            st.mark(v.reciprocal(lb_sb[:, 1, :], lb_sb[:, 0, :]))
            st.wait()
            hvec = head_vec.rearrange("p (r n) -> p r n", n=3)
            st.mark(v.tensor_tensor(hvec[:, 0:NH, 0], lb_t[:, 0, :], lb_sb[:, 1, :], ALU.mult))
            st.wait()
            st.mark(v.tensor_scalar(hvec[:, 0:NH, 1], hvec[:, 0:NH, 0], -1.0, 1.0, ALU.mult, ALU.add))
            st.mark(v.memset(hv_now[:, :], 0.0))
            st.fresh()
            with vec_e.Fori(0, HALVES) as h:
                st.mark(v.memset(attn, 0.0))
                for s in out_stored:
                    vec_e.wait_ge(s, h * 64 + 16)
                v.memset(t1, 0.0).then_inc(t1_zero, 1)
                vec_e.wait_ge(xss_ready, h + 1)
                st.mark(v.tensor_reduce(x_var, x_ss.rearrange("p (t a) -> p t a", a=4), AX.X, ALU.add))
                st.wait()
                v.tensor_scalar(x_var, x_var, 1.0 / D, EPS, ALU.mult, ALU.add).then_inc(xvar_ready, 1)
                vec_e.wait_ge(xy0_ready, h + 1)
                st.mark(newton(x_r, x_r, x_var, x_tmp))
                st.wait()
                for t in range(4):
                    v.tensor_scalar(x_in[:, t, :], x_in[:, t, :], x_r[:, t:t + 1], None, ALU.mult
                                    ).then_inc(xn_ready, 1)
                ring = [lv_ps[0], lv_ps[1], so_ps[0], so_ps[1], tr_ps]
                vec_e.wait_ge(acc_ready, h * TILES + 2)
                for k in range(KT):
                    vec_e.wait_ge(act_hi_ready, h * (3 * KT) + (k + 1))
                    v.scalar_tensor_tensor(out=act_lo[:, k, :], in0=ring[k % 5][:, :], scalar=nmix[:, k:k + 1],
                                           in1=act_hi[:, k, :].bitcast(F32), op0=ALU.mult, op1=ALU.subtract
                                           ).then_inc(act_lo_ready, 1)
                hgrn_iteration(h, 0, False)
                st.fresh()
                with vec_e.Fori(1, NH) as n:
                    hgrn_iteration(h, n, True)
                    st.fresh()
                gla_iteration(h, 0, 1)
                st.fresh()
                with vec_e.Fori(1, NG) as m:
                    gla_iteration(h, m, 2)
                    st.fresh()
                R = h * HEADS + (HEADS - 1)
                st.mark(v.tensor_copy(hv_rec[:, 0:3], hv_now[:, 0:3]))
                rec_first(h, R, 3 * HEADS - 1, 3 * NH + 2 * NG - 1, zs[:, TH:2 * TH])
                for k in range(2):
                    vec_e.wait_ge(pT_hi, h * 2 + (k + 1))
                    v.tensor_tensor(act_lo[:, KT - 2 + k, :], (tr_ps, ms_ps)[k][:, :],
                                    act_hi[:, KT - 2 + k, :].bitcast(F32), ALU.subtract).then_inc(pT_lo, 1)
                state_chain(R, 2, state_g[:, (NG - 1) * 2 * P:NG * 2 * P])
                st.mark(v.memset(sq_sum[:, :], 0.0))
                after = {0: 0, 1: 1, 3: 2, 4: 3, 6: 4}
                for e in range(E_TILES):
                    vec_e.wait_ge(e_sq, h * E_TILES + (e + 1))
                    if e:
                        vec_e.wait_ge(e_added, h * E_TILES + e)
                    else:
                        st.wait()
                    v.tensor_tensor(sq_sum[:, :], sq_sum[:, :], (t1, t2)[e % 2], ALU.add).then_inc(e_added, 1)
                    if e in after:
                        next_level(R, after[e])
                    if e in (8, 9):
                        mask_level(R, e - 3)
                    if e == 12:
                        o_copy(R, 2)
                    if e == 13:
                        o_norm(R, 2)
                y_out(R, 2, 2 * (NG - 1) + NH, 1)
                st.fresh()
                for k in range(KT):
                    vec_e.wait_ge(act_hi_ready, h * (3 * KT) + (KT + k + 1))
                    v.tensor_tensor(act_lo[:, k, :], feat[:, k, :], act_hi[:, k, :].bitcast(F32), ALU.subtract
                                    ).then_inc(act_lo_ready, 1)

                def row_factors(no, dst):
                    vec_e.wait_ge(rows_ready, no)
                    v.tensor_scalar(t1, ms_ps[:, :], 1.0 / D, EPS, ALU.mult, ALU.add).then_inc(rvar_ready, 1)
                    st.mark(v.memset(sq_sum[:, :], 0.0))
                    vec_e.wait_ge(ry0_ready, no)
                    st.mark(newton(dst, t2, t1, g_t))
                    st.wait()

                row_factors(h * 2 + 1, r_e[:, :])
                st.fresh()
                with vec_e.Fori(0, KT // 2) as i:
                    for par in range(2):
                        c = i * 2 + par
                        vec_e.wait_ge(acc_ready, tile_done(h, c + O_TILE))
                        vec_e.wait_ge(xt_copied, h * KT + (c + 3))
                        v.tensor_tensor(h_sb[par], acc[par][:, :], xt_sb[par], ALU.add).then_inc(acc_free[par], 1)
                        vec_e.wait_ge(acc_free[par], tile_free(h, i + O_TILE // 2))
                        v.tensor_copy(feat[:, bass.ds(c, 1), :].rearrange("p o n -> p (o n)"), h_sb[par]
                                      ).then_inc(h1_ready, 1)
                        vec_e.wait_ge(h_sq, h * KT + (c + 1))
                        v.tensor_tensor(sq_sum[:, :], sq_sum[:, :], (t1, t2)[par], ALU.add).then_inc(h_added, 1)
                        vec_e.wait_ge(h_added, h * KT + (c + 1))
                for k in range(KT):
                    vec_e.wait_ge(act_hi_ready, h * (3 * KT) + (2 * KT + k + 1))
                    v.scalar_tensor_tensor(out=act_lo[:, k, :], in0=feat[:, k, :], scalar=pgn[:, k:k + 1],
                                           in1=act_hi[:, k, :].bitcast(F32), op0=ALU.mult, op1=ALU.subtract
                                           ).then_inc(act_lo_ready, 1)
                row_factors(h * 2 + 2, r_h[:, :])
                st.fresh()
                with vec_e.Fori(0, KT // 2) as i:
                    for par in range(2):
                        c = i * 2 + par
                        gv = gv_now[:, par, :]
                        st.mark(v.tensor_copy(gv[:, 0:3], g_vec[:, bass.ds(c * 3, 3)]))
                        vec_e.wait_ge(acc_ready, tile_done(h, c + G_TILE))
                        v.tensor_tensor(g_t, acc[par][:, :], r_h[:, :], ALU.mult).then_inc(acc_free[par], 1)
                        vec_e.wait_ge(acc_free[par], tile_free(h, i + G_TILE // 2))
                        v.tensor_scalar(g_t, g_t, gv[:, 0:1], None, ALU.add).then_inc(g_arg, 1)
                        vec_e.wait_ge(e_loaded[par], h * 128 + (i * 16 + 16))
                        v.scalar_tensor_tensor(out=g_m, in0=e_in[par], scalar=gv[:, 1:2], in1=r_e[:, :],
                                               op0=ALU.mult, op1=ALU.mult).then_inc(e_used, 1)
                        vec_e.wait_ge(e_used, h * KT + (c + 1))
                        log_sigmoid(h, c + 3 * HEADS, g_t)
                        vec_e.wait_ge(sig_ready, h * SIGMOIDS + (c + (3 * NH + 2 * NG + 1)))
                        st.mark(v.tensor_tensor(g_m, g_m, t2, ALU.mult))
                        st.wait()
                        v.tensor_tensor(g_t, feat[:, bass.ds(c, 1), :].rearrange("p o n -> p (o n)"), g_m, ALU.add
                                        ).then_inc(g2_sum, 1)
                        vec_e.wait_ge(g2_sum, h * KT + (c + 1))
                        st.mark(v.tensor_scalar(feat[:, bass.ds(c, 1), :].rearrange("p o n -> p (o n)"), g_t,
                                                gv[:, 2:3], None, ALU.mult))
                        vec_e.wait_ge(g2_sq, h * KT + (c + 1))
                        v.tensor_tensor(sq_sum[:, :], sq_sum[:, :], t1, ALU.add).then_inc(g2_ready, 1)
                        vec_e.wait_ge(g2_ready, h * KT + (c + 1))
                    st.fresh()
                vec_e.wait_ge(fsum_ready, h + 1)
                v.tensor_scalar(f_var, ms_ps[:, 0:4], 1.0 / D, EPS, ALU.mult, ALU.add).then_inc(fvar_ready, 1)
                vec_e.wait_ge(fy0_ready, h + 1)
                st.mark(newton(f_r, f_r, f_var, f_tmp))
                st.wait()
                banks = [lv_ps[0], lv_ps[1], so_ps[0], so_ps[1]]
                for n in range(16):
                    vec_e.wait_ge(ft_ready, h * 16 + (n + 1))
                    vec_e.wait_ge(out_stored[n % 4], h * 64 + (16 * (n // 4) + 16))
                    v.tensor_scalar(stage[n % 4], banks[n % 4][:, :], f_r[:, n // 4:n // 4 + 1], None, ALU.mult
                                    ).then_inc(ft_copied, 1)
                st.fresh()


def level_masks():
    j = np.arange(C)[:, None]
    out = np.zeros((C, LEVELS, NC_, C // 2), np.float32)
    for l in range(LEVELS):
        s = 1 << l
        u = np.arange(C // 2)[None, :]
        block = u // s
        out[:, l, :, :] = ((j // (2 * s) == block) & (j % (2 * s) < s))[:, None, :]
    return out.reshape(C, LEVELS * NC_ * C // 2)


def kernel(**inputs):
    import concourse.bacc as bacc
    from concourse.bass_utils import run_bass_kernel_spmd

    a = {k: np.asarray(v) for k, v in inputs.items()}
    w_in = a["w_in"][0]

    def slab_of(w, c0):
        return w[:, c0:c0 + P].reshape(2, KT // 2, P, P).transpose(0, 2, 1, 3).reshape(2, P, 1024)

    ple = a["ple_proj"][0].reshape(2, P, 2, 1024)
    slabs = np.stack([slab_of(w_in, c) for c in slab_columns()]
                     + [ple[:, :, e, :] for e in range(2)]
                     + [slab_of(a["w_out"][0], c * P) for c in range(KT)]
                     + [slab_of(a["ple_gate_w"][0], c * P) for c in range(KT)])

    def by_tile(w):
        return w.reshape(-1, P).T

    head_vec = np.zeros((P, HEADS, 3), np.float32)
    head_vec[:, :NH, 2] = by_tile(a["hgrn_norm_w"][0])
    head_vec[:, NH:, 0] = by_tile(a["gla_gate_b"][0])
    head_vec[:, NH:, 1:] = by_tile(a["gla_norm_w"][0]).reshape(P, NG, 2)
    g_vec = np.stack([by_tile(a["ple_gate_b"][0]), by_tile(a["ple_norm_w"][0]), by_tile(a["final_norm_w"])], axis=2)
    vec = np.concatenate([by_tile(a["norm_mix_w"][0]), by_tile(a["ple_gate_norm_w"][0]),
                          head_vec.reshape(P, -1), g_vec.reshape(P, -1)], axis=1)
    restart = np.ones((P, TH), np.float32)
    restart[:, ::C] = 0.0
    arrays = {
        "x": a["x"].reshape(HALVES, 4, P, D),
        "p": a["p"].reshape(HALVES, 4, P, PLE).transpose(0, 2, 1, 3),
        "slabs": slabs,
        "w_glr": w_in[:, -RANK:].reshape(KT, P, RANK).transpose(1, 0, 2).reshape(P, KT * RANK),
        "w2": np.concatenate([a["gla_gate_w2"][0]] * 2, axis=0),
        "vec": vec,
        "lb_rows": a["hgrn_lb"].reshape(2, NH, P).transpose(2, 0, 1),
        "masks": level_masks(),
        "restart": restart,
        "ident": np.eye(P, dtype=np.float32),
    }
    arrays = {k: np.ascontiguousarray(v) for k, v in arrays.items()}
    nc = bacc.Bacc("TRN2", target_bir_lowering=False, num_devices=1)
    aps = [nc.dram_tensor(f"in_{k}", v.shape, mybir.dt.from_np(v.dtype), kind="ExternalInput").ap() for k, v in arrays.items()]
    out = nc.dram_tensor("out", (HALVES, 4, P, D), F32, kind="ExternalOutput").ap()
    e_scratch = nc.dram_tensor("e_scratch", (E_TILES, P, TH), F32, kind="Internal").ap()
    build(nc, *aps, out, e_scratch)
    r = run_bass_kernel_spmd(nc, [{f"in_{k}": v for k, v in arrays.items()}], core_ids=[0])
    return r.results[0]["out"].reshape(1, SEQ, D)
```

```python
from contextlib import ExitStack

import numpy as np
import concourse.bass as bass
from concourse import mybir

F32 = mybir.dt.float32
F32R = mybir.dt.float32r
U8 = mybir.dt.uint8
ALU = mybir.AluOpType
ACT = mybir.ActivationFunctionType
AX = mybir.AxisListType

P = 128
SEQ, D = 1024, 2048
KT = D // P
HALVES = 2
TH = SEQ // HALVES
C = 128
NC_ = TH // C
LEVELS = 7
NH, NG = 8, 4
HEADS = NH + NG
PLE = 256
RANK = 16
EPS = 1e-6
SCALE = float(P) ** -0.5
TAU = 16.0
LN_MIN = 1e-19
D_H = D // 2

SLABS_H, SLABS_G = 4, 6
I_SLABS = NH * SLABS_H + NG * SLABS_G
E_SLABS, E_TILES = 2, KT
O_SLAB = I_SLABS + E_SLABS
G_SLAB = O_SLAB + KT
SLABS = G_SLAB + KT
E_TILE = I_SLABS
O_TILE = E_TILE + E_TILES
G_TILE = O_TILE + KT
TILES = G_TILE + KT
assert SLABS % 2 == 0 and TILES % 2 == 0
SIGS = 3 * HEADS + KT
SIGMOIDS = 3 * NH + 2 * NG + KT


def slab_columns():
    hq, hf, hi, hz = (i * D_H for i in range(4))
    gq = 4 * D_H
    gk = gq + NG * P
    gv = gk + NG * P
    gz = gv + D_H
    cols = []
    for n in range(NH):
        cols += [hi + n * P, hf + n * P, hq + n * P, hz + n * P]
    for m in range(NG):
        cols += [gv + 2 * m * P, gv + (2 * m + 1) * P, gk + m * P, gq + m * P,
                 gz + 2 * m * P, gz + (2 * m + 1) * P]
    return cols


class Steps:

    def __init__(self, eng, sem, spacer):
        self.eng, self.sem, self.n, self.spacer = eng, sem, 0, spacer

    def mark(self, ins):
        ins.then_inc(self.sem, 1)
        self.n += 1

    def wait(self):
        if self.n:
            self.eng.wait_ge(self.sem, self.n)

    def space(self):
        self.wait()
        self.mark(self.spacer())

    def fresh(self):
        self.space()
        if self.n:
            self.eng.wait_ge(self.sem, self.n)
            self.eng.sem_clear(self.sem)
            self.n = 0


def build(nc, x, x_feat, p, slabs, w_glr, w2, vec, lb_rows, masks, restart, ident_d, out, e_scratch):
    with ExitStack() as ctx:
        def sb(name, shape, dt=F32):
            return ctx.enter_context(nc.sbuf_tensor(name, shape, dt))

        def sem(name):
            return ctx.enter_context(nc.semaphore(name))

        act_hi = sb("act_hi", [P, KT, TH], F32R)
        act_lo = sb("act_lo", [P, KT, TH], F32R)
        feat = sb("feat", [P, KT, TH])
        w_hi = [sb(f"w_hi{i}", [P, 2, 1024], F32R) for i in range(2)]
        w_lo = [sb(f"w_lo{i}", [P, 2, 1024], F32R) for i in range(2)]
        w_raw = [sb(f"w_raw{j}", [P, 1024]) for j in range(2)]
        work = sb("work", [P, 22, TH])

        def unit(i, n=1):
            v = work[:, i:i + n, :]
            return v.rearrange("p n t -> p (n t)")

        v_feat = unit(0, 2)
        q_t, k_t, b_t = unit(2), unit(3), unit(4)
        qb, kt = unit(5), unit(6)
        junk = unit(5, 2)
        kt_pos = unit(7)
        v_pos = unit(8, 2)
        on_pos = unit(10, 2)
        zs = unit(12, 2)
        s_in = unit(14, 2)
        qk = unit(21)
        attn = unit(16)
        t1, t2 = unit(17), unit(18)
        x_lv = [unit(19), unit(20)]
        mask_f32 = work[:, 17:21, :].rearrange("p n t -> p (n t)")[:, 0:LEVELS * TH // 2]
        glr_raw = work[:, 17:21, :].rearrange("p n t -> p (n t)")[:, 4 * TH - KT * RANK:]
        x_in = work[:, 0:16, :].rearrange("p (t a) n -> p t (a n)", t=4)
        p_raw = unit(10, 2)
        e_buf = [unit(0), unit(1)]
        z_last = zs[:, TH:2 * TH]
        y_high_at = {13: 12, 14: 13}
        y_low_at = {1: 6, 2: 7, 4: 8, 6: 9, 8: 10, 9: 11, 13: 12, 14: 13}
        xt_sb = [unit(2), unit(3)]
        h_sb = [unit(4), unit(5)]
        e_in = [unit(16), unit(19)]
        g_t, g_m = unit(20), unit(21)
        f_var, f_y0, f_tmp = unit(7), unit(5), unit(6)

        sq_sum = sb("sq_sum", [P, TH])
        r_e = sb("r_e", [P, TH])
        glr_t = sb("glr_t", [P, TH])
        r_h = glr_t
        sq_e = [r_e[:, :], qk]
        w2_sb = sb("w2_sb", [P, NG * P])
        w2_now = sb("w2_now", [P, P])
        restart_sb = sb("restart_sb", [P, TH])
        mask_sb = sb("mask_sb", [P, LEVELS, TH // 2], U8)
        ident = sb("ident", [P, P])
        ones = sb("ones", [P, P])
        glr_all = sb("glr_all", [P, KT * 2 * RANK + P - 2 * RANK], F32R)
        glr_w = glr_all[:, 0:KT * 2 * RANK].rearrange("p (k n) -> p k n", n=2 * RANK)
        state_h = sb("state_h", [P, NH * P])
        state_g = sb("state_g", [P, NG * 2 * P])
        vecs = sb("vecs", [P, 32 + 3 * HEADS + 3 * KT])
        nmix = vecs[:, 0:16]
        pgn = vecs[:, 16:32]
        head_vec = vecs[:, 32:32 + 3 * HEADS]
        g_vec = vecs[:, 32 + 3 * HEADS:32 + 3 * HEADS + 3 * KT]
        lb_sb = sb("lb_sb", [P, 2, NH])
        lb_t = sb("lb_t", [P, 2, NH])
        hv_now = sb("hv_now", [P, 4])
        hv_rec = sb("hv_rec", [P, 4])
        gv_now = sb("gv_now", [P, 2, 4])
        small = sb("small", [P, 64])
        vec_dummy, act_dummy = sb("vec_dummy", [P, 1]), sb("act_dummy", [P, 1])
        x_ss, x_var, x_r, x_tmp = small[:, 0:16], small[:, 16:20], small[:, 20:24], small[:, 24:28]
        e_last, diag = small[:, 28:32], small[:, 32:36]
        o_ss, o_var, o_r, o_tmp = small[:, 36:40], small[:, 40:44], small[:, 44:48], small[:, 48:52]
        f_r = sq_sum[:, :]

        def bank(name):
            return ctx.enter_context(nc.psum_tensor(name, [P, 512], F32))

        acc = [bank("acc0"), bank("acc1")]
        lv_ps = [bank("lv0"), bank("lv1")]
        so_ps = [bank("so0"), bank("so1")]
        tr_ps, ms_ps = bank("tr"), bank("ms")

        const_loaded, glrw_loaded = sem("const_loaded"), sem("glrw_loaded")
        const_ready = sem("const_ready")
        lb_arg, lb_exp = sem("lb_arg"), sem("lb_exp")
        first_loaded = sem("first_loaded")
        x_loaded = [sem(f"x_loaded{i}") for i in range(4)]
        x_end_loaded = sem("x_end_loaded")
        raw_loaded = [sem("raw_loaded0"), sem("raw_loaded1")]
        w_hi_ready, w_lo_ready = sem("w_hi_ready"), sem("w_lo_ready")
        act_hi_ready, act_lo_ready = sem("act_hi_ready"), sem("act_lo_ready")
        xt_ready = sem("xt_ready")
        xss_ready, xvar_ready, xy0_ready, xn_ready = (sem(s) for s in ("xss_ready", "xvar_ready", "xy0_ready", "xn_ready"))
        glr_ready, glrt_ready, glrw_hi = sem("glr_ready"), sem("glrt_ready"), sem("glrw_hi")
        glrw_ready = sem("glrw_ready")
        act_free = sem("act_free")
        h1_ready, g_arg = sem("h1_ready"), sem("g_arg")
        acc_ready = sem("acc_ready")
        acc_free = [sem("acc_free0"), sem("acc_free1")]
        sp_ready, ls_ready, sig_ready = sem("sp_ready"), sem("ls_ready"), sem("sig_ready")
        f_ready, g_ready = sem("f_ready"), sem("g_ready")
        logit_ready = sem("logit_ready")
        hv_ready = sem("hv_ready")
        vtr_ready, v_ready = sem("vtr_ready"), sem("v_ready")
        kt_arg, kt_exp, kt_ready = sem("kt_arg"), sem("kt_exp"), sem("kt_ready")
        qb_exp, qb_ready, elast_ready = sem("qb_exp"), sem("qb_ready"), sem("elast_ready")
        qk_ready, dgps_ready, dg_ready = sem("qk_ready"), sem("dgps_ready"), sem("dg_ready")
        kttr_ready, ktpos_ready = sem("kttr_ready"), sem("ktpos_ready")
        su_ready, s_ready = sem("su_ready"), sem("s_ready")
        lv_arg, lv_exp, lv_in = sem("lv_arg"), sem("lv_exp"), sem("lv_in")
        lv_ready, masked = sem("lv_ready"), sem("masked")
        o_ready, o_copied, oss_ready = sem("o_ready"), sem("o_copied"), sem("oss_ready")
        ovar_ready, oy0_ready, on_ready = sem("ovar_ready"), sem("oy0_ready"), sem("on_ready")
        ontr_ready, y_ready = sem("ontr_ready"), sem("y_ready")
        p_loaded, pT_hi, pT_lo = sem("p_loaded"), sem("pT_hi"), sem("pT_lo")
        e_sq, e_added = sem("e_sq"), sem("e_added")
        e_stored = [sem("e_stored0"), sem("e_stored1")]
        e_loaded = [sem("e_loaded0"), sem("e_loaded1")]
        e_used = sem("e_used")
        rows_ready, rvar_ready, ry0_ready = sem("rows_ready"), sem("rvar_ready"), sem("ry0_ready")
        xb_loaded = [sem("xb_loaded0"), sem("xb_loaded1")]
        h_sq, h_added = sem("h_sq"), sem("h_added")
        g2_sq, g2_sum, g2_ready = sem("g2_sq"), sem("g2_sum"), sem("g2_ready")
        fsum_ready, fvar_ready, fy0_ready = (sem(s) for s in ("fsum_ready", "fvar_ready", "fy0_ready"))
        f_scaled, out_stored = sem("f_scaled"), sem("out_stored")
        act_steps, vec_steps = sem("act_steps"), sem("vec_steps")

        def tile_done(h, o):
            return h * TILES + (o + 3)

        def tile_free(h, half_no):
            return h * (TILES // 2) + (half_no + 2)

        block = ctx.enter_context(nc.Block())

        @block.sync
        def _(sp):
            for t in range(3):
                sp.dma_start(x_in[:, t, :], x[0, t]).then_inc(x_loaded[t], 16)
            sp.dma_start(x_in[:, 3, 0:D // 2], x[0, 3][:, 0:D // 2]).then_inc(x_loaded[3], 16)
            sp.dma_start(x_in[:, 3, D // 2:D], x[0, 3][:, D // 2:D]).then_inc(x_end_loaded, 16)
            for dst, src in ((ident[:, :], ident_d), (vecs[:, :], vec)):
                sp.dma_start(dst, src).then_inc(first_loaded, 16)

            def load_constants():
                for dst, src in ((lb_sb[:, :, :], lb_rows), (w2_sb[0:2 * RANK, :], w2),
                                 (mask_f32, masks), (restart_sb[:, :], restart)):
                    sp.dma_start(dst, src).then_inc(const_loaded, 16)
                sp.dma_start(glr_raw, w_glr).then_inc(glrw_loaded, 16)

            def load_slab(h, s):
                g = h * SLABS + s
                for j in range(2):
                    sp.wait_ge(w_lo_ready, g * 2 + (j + 1))
                    sp.dma_start(w_raw[j][:, :], slabs[bass.ds(s, 1), j, :, :].rearrange("o p n -> (o p) n")
                                 ).then_inc(raw_loaded[j], 16)

            def store_out(h, n):
                sp.wait_ge(f_scaled, h * KT + (n + 1))
                sp.dma_start(out[h, n], feat[:, n, :]).then_inc(out_stored, 16)

            for h in range(HALVES):
                first_slabs = 5
                for s in range(first_slabs):
                    load_slab(h, s)
                    if h == 0 and s == 0:
                        load_constants()
                    if h and s >= 3:
                        for n in (range(8) if s == 3 else range(8, 16)):
                            store_out(h - 1, n)
                with sp.Fori(first_slabs, I_SLABS) as s:
                    load_slab(h, s)
                sp.wait_ge(ontr_ready, h * HEADS + (HEADS - 1))
                sp.dma_start(p_raw, p[h]).then_inc(p_loaded, 16)
                load_slab(h, I_SLABS)
                load_slab(h, I_SLABS + 1)

                def store_e(e):
                    sp.wait_ge(acc_free[e % 2], tile_free(h, (E_TILE + e) // 2))
                    sp.dma_start(e_scratch[e], e_buf[e % 2]).then_inc(e_stored[e % 2], 16)

                for e in range(E_TILES):
                    store_e(e)
                    if e in (3, 13):
                        load_slab(h, O_SLAB + (e == 13))
                for u in range(2):
                    sp.wait_ge(e_stored[u], h * 128 + 128)

                def load_x_tile(i, par, wait):
                    if wait:
                        sp.wait_ge(acc_free[par], tile_free(h, i + (O_TILE // 2 - 1)))
                    sp.dma_start(xt_sb[par], x_feat[h, bass.ds(i * 2 + par, 1), :, :].rearrange("o p n -> (o p) n")
                                 ).then_inc(xb_loaded[par], 16)

                load_x_tile(0, 0, False)
                load_x_tile(0, 1, False)
                load_slab(h, O_SLAB + 2)
                with sp.Fori(0, (KT - 2) // 2) as i:
                    for par in range(2):
                        load_x_tile(i + 1, par, True)
                        load_slab(h, i * 2 + (O_SLAB + 3 + par))
                sp.wait_ge(h_added, h * KT + KT)

                def load_e(c, par, wait):
                    if wait:
                        sp.wait_ge(e_used, h * KT + (c - 1))
                    sp.dma_start(e_in[par], e_scratch[bass.ds(c, 1), :, :].rearrange("o p n -> (o p) n")
                                 ).then_inc(e_loaded[par], 16)

                load_e(0, 0, False)
                load_e(1, 1, False)
                load_slab(h, G_SLAB + 1)
                for c in range(2, 6):
                    load_slab(h, G_SLAB + c)
                    load_e(c, c % 2, True)
                    if h < HALVES - 1:
                        sp.dma_start(x_in[:, c - 2, :], x[h + 1, c - 2]).then_inc(x_loaded[c - 2], 16)
                with sp.Fori(2, (KT - 2) // 2) as i:
                    for par in range(2):
                        load_slab(h, i * 2 + (G_SLAB + 2 + par))
                        load_e(i * 2 + (2 + par), par, True)
            for n in range(16):
                store_out(HALVES - 1, n)
            sp.wait_ge(out_stored, HALVES * KT * 16)

        @block.gpsimd
        def _(pool):
            for s, credit in ((w_lo_ready, 2), (acc_ready, 2), (acc_free[0], 1), (acc_free[1], 1),
                              (ls_ready, 1), (o_copied, 1), (y_ready, 1), (masked, 2)):
                pool.sem_inc(s, credit)

            with pool.Fori(0, HALVES * SLABS // 2) as i:
                for par in range(2):
                    for j in range(2):
                        pool.wait_ge(w_hi_ready, i * 4 + (2 * par + j + 1))
                        nc.gpsimd.tensor_tensor(w_lo[par][:, j, :], w_raw[j][:, :],
                                                w_hi[par][:, j, :].bitcast(F32), ALU.subtract
                                                ).then_inc(w_lo_ready, 1)

        @block.tensor
        def _(pe):
            def passes(ps, lhs_hi, lhs_lo, rhs_hi, rhs_lo, start, stop):
                nc.tensor.matmul(ps, lhs_lo, rhs_hi, start=start, stop=False)
                nc.tensor.matmul(ps, lhs_hi, rhs_lo, start=False, stop=False)
                return nc.tensor.matmul(ps, lhs_hi, rhs_hi, start=False, stop=stop)

            def slab(h, s, par, half_no, hooks=None, act_from=None, last_use=False,
                     ends_first=False):
                hooks = hooks or {}
                pe.wait_ge(acc_free[par], h * (TILES // 2) + (half_no + 1))
                g = h * SLABS + s
                order = [KT - 2, KT - 1] + list(range(KT - 2)) if ends_first else list(range(KT))
                for step, k in enumerate(order):
                    if step % 8 == 0:
                        half = 1 if ends_first else step // 8
                        pe.wait_ge(w_hi_ready, g * 2 + (half + 1))
                        pe.wait_ge(w_lo_ready, g * 2 + (half + 3))
                    if act_from is not None:
                        pe.wait_ge(act_hi_ready, h * (3 * KT) + (act_from + k + 1))
                        pe.wait_ge(act_lo_ready, h * (3 * KT) + (act_from + k + 1))
                    cols = slice((k % 8) * P, (k % 8 + 1) * P)
                    last = passes(acc[par][:, :], w_hi[par][:, k // 8, cols], w_lo[par][:, k // 8, cols],
                                  act_hi[:, k, :], act_lo[:, k, :], step == 0, step == KT - 1)
                    if step == KT - 1:
                        last.then_inc(acc_ready, 1)
                    elif last_use and k % 4 == 3:
                        last.then_inc(act_free, 1)
                    if step in hooks:
                        hooks[step]()

            def v_transpose(R, nb, h, half_no):
                pe.wait_ge(glrt_ready, h + 1)
                pe.wait_ge(acc_free[nb - 1], tile_free(h, half_no))
                pe.wait_ge(y_ready, R + 1)
                for vb in range(nb):
                    for c in range(NC_):
                        last = nc.tensor.transpose((tr_ps, ms_ps)[vb][:, c * P:(c + 1) * P],
                                                   v_feat[:, vb * TH + c * C:vb * TH + (c + 1) * C], ident[:, :])
                last.then_inc(vtr_ready, 1)

            def k_transpose(R):
                pe.wait_ge(kt_ready, R + 1)
                pe.wait_ge(v_ready, R + 1)
                for c in range(NC_):
                    last = nc.tensor.transpose(tr_ps[:, c * P:(c + 1) * P], kt[:, c * C:(c + 1) * C], ident[:, :])
                last.then_inc(kttr_ready, 1)
                pe.wait_ge(qk_ready, R + 1)
                for c in range(NC_):
                    last = nc.tensor.matmul(ms_ps[:, c:c + 1], qk[:, c * C:(c + 1) * C], ones[:, 0:1],
                                            start=True, stop=True)
                last.then_inc(dgps_ready, 1)

            def so_view(nb, c):
                return so_ps[(c * nb) // NC_][:, (c * nb) % NC_ * P:((c * nb) % NC_ + nb) * P]

            def state_update(R, nb):
                pe.wait_ge(ktpos_ready, R + 1)
                pe.wait_ge(o_copied, R + 1)
                for c in range(NC_):
                    last = nc.tensor.matmul(so_view(nb, c), kt_pos[:, c * P:(c + 1) * P],
                                            v_pos[:, c * nb * P:(c + 1) * nb * P], start=True, stop=True)
                last.then_inc(su_ready, 1)

            def level(R, l):
                pe.wait_ge(lv_in, R * LEVELS + (l + 1))
                pe.wait_ge(masked, R * LEVELS + (l + 1))
                s = 1 << l
                for c in range(NC_):
                    xc = x_lv[l % 2][:, c * C:(c + 1) * C]
                    upper = xc.rearrange("p (n two s) -> p n two s", two=2, s=s)[:, :, 1, :]
                    last = nc.tensor.matmul(lv_ps[l % 2][:, c * 64:(c + 1) * 64].rearrange("p (n s) -> p n s", s=s),
                                            xc, upper, start=True, stop=True)
                last.then_inc(lv_ready, 1)

            def readout(R, nb):
                pe.wait_ge(masked, R * LEVELS + (LEVELS + 2))
                pe.wait_ge(s_ready, R + 1)
                pe.wait_ge(qb_ready, R + 1)
                for c in range(NC_):
                    nc.tensor.matmul(so_view(nb, c), attn[:, c * C:(c + 1) * C],
                                     v_pos[:, c * nb * P:(c + 1) * nb * P], start=True, stop=False)
                    last = nc.tensor.matmul(so_view(nb, c), qb[:, c * C:(c + 1) * C],
                                            s_in[:, c * nb * P:(c + 1) * nb * P], start=False, stop=True)
                last.then_inc(o_ready, 1)

            def o_transpose(R, nb, logit_no=None):
                pe.wait_ge(on_ready, R + 1)
                if logit_no is not None:
                    pe.wait_ge(ls_ready, logit_no)
                for vb in range(nb):
                    for c in range(NC_):
                        last = nc.tensor.transpose((tr_ps, ms_ps)[vb][:, c * P:(c + 1) * P],
                                                   on_pos[:, (c * nb + vb) * P:(c * nb + vb + 1) * P], ident[:, :])
                last.then_inc(ontr_ready, 1)

            def gate_logits(R, m):
                pe.wait_ge(dg_ready, R)
                pe.wait_ge(hv_ready, R + 1)
                nc.tensor.matmul(ms_ps[:, :], w2_now[0:2 * RANK, :], glr_t[0:2 * RANK, :],
                                 start=True, stop=True).then_inc(logit_ready, 1)

            def levels(R, ls):
                return {k: (lambda l=l: level(R, l)) for k, l in ls}

            def hgrn_iteration(h, n, rec, first_hooks=None):
                r0 = h * HEADS + n
                hooks = first_hooks or [{}, {}, {}, {}]
                if rec:
                    R = r0 - 1
                    hooks[0] = {7: lambda: k_transpose(R), 15: lambda: state_update(R, 1)}
                    hooks[1] = levels(R, ((2, 0), (6, 1), (10, 2), (14, 3)))
                    hooks[2] = levels(R, ((2, 4), (6, 5), (10, 6)))
                    hooks[3] = {1: lambda: readout(R, 1), 11: lambda: o_transpose(R, 1)}
                hooks[3][15] = lambda: v_transpose(r0, 1, h, n * 2)
                for j in range(SLABS_H):
                    slab(h, n * SLABS_H + j, j % 2, n * 2 + j // 2, hooks[j],
                         0 if (not rec and j == 0) else None)

            def gla_iteration(h, m, rec_nb, last=False):
                r0 = h * HEADS + (m + NH)
                R = r0 - 1
                hooks = [{7: lambda: k_transpose(R), 15: lambda: state_update(R, rec_nb)},
                         levels(R, ((2, 0), (6, 1), (10, 2), (14, 3))),
                         levels(R, ((2, 4), (6, 5), (10, 6))),
                         {1: lambda: gate_logits(r0, m), 7: lambda: readout(R, rec_nb)},
                         {13: lambda: o_transpose(R, rec_nb, (h * SIGS + (m * 3 + (3 * NH + 2))))}, {}]

                def own_v():
                    v_transpose(r0, 2, h, m * 3 + NH * SLABS_H // 2)

                if last:
                    hooks[4][11] = hooks[4].pop(13)
                    hooks[4].update(levels(r0, ((14, 0),)))
                    hooks[5] = levels(r0, ((3, 1), (6, 2), (10, 3), (13, 4)))
                    hooks[5][1] = own_v
                    hooks[5][5] = lambda: k_transpose(r0)
                    hooks[5][8] = lambda: state_update(r0, 2)
                else:
                    hooks[5][11] = own_v
                for j in range(SLABS_G):
                    slab(h, m * SLABS_G + (NH * SLABS_H + j), j % 2,
                         m * 3 + (NH * SLABS_H // 2 + j // 2), hooks[j],
                         last_use=last and j == SLABS_G - 1, ends_first=last and j == SLABS_G - 1)

            pe.wait_ge(first_loaded, 16 * 2)
            pe.wait_ge(const_ready, 1)
            ring = [lv_ps[0], lv_ps[1], so_ps[0], so_ps[1], tr_ps]

            def transpose_x(h, k):
                if k >= len(ring):
                    pe.wait_ge(act_lo_ready, h * (3 * KT) + (k - len(ring) + 1))
                    pe.wait_ge(act_hi_ready, h * (3 * KT) + (k - len(ring) + 1))
                elif k == 0:
                    pe.wait_ge(xn_ready, h * 4 + 4)
                for t in range(4):
                    last = nc.tensor.transpose(ring[k % len(ring)][:, t * P:(t + 1) * P],
                                               x_in[:, t, k * P:(k + 1) * P], ident[:, :])
                last.then_inc(xt_ready, 1)

            def row_sums(h):
                pe.wait_ge(g2_ready, h * KT + KT)
                nc.tensor.matmul(ms_ps[:, :], ones[:, :], sq_sum[:, :], start=True, stop=True).then_inc(fsum_ready, 1)

            def glr_product(h):
                if h:
                    pe.wait_ge(fvar_ready, h)
                pe.wait_ge(glrw_ready, 1)
                for k in range(KT):
                    nc.tensor.matmul(ms_ps[:, :], glr_all[:, k * 2 * RANK:k * 2 * RANK + P], act_lo[:, k, :], start=(k == 0), stop=False)
                    last = nc.tensor.matmul(ms_ps[:, :], glr_all[:, k * 2 * RANK:k * 2 * RANK + P], act_hi[:, k, :], start=False, stop=(k == KT - 1))
                last.then_inc(glr_ready, 1)

            for k in range(len(ring)):
                transpose_x(0, k)
            for h in range(HALVES):
                hooks = [{k: (lambda k=k: transpose_x(h, k + len(ring))) for k in range(KT - len(ring))},
                         {15: lambda: glr_product(h)}, {}, {}]
                if h:
                    hooks[1][6] = lambda: row_sums(h - 1)
                hgrn_iteration(h, 0, False, hooks)
                with pe.Fori(1, NH) as n:
                    hgrn_iteration(h, n, True)
                gla_iteration(h, 0, 1)
                with pe.Fori(1, NG - 1) as m:
                    gla_iteration(h, m, 2)
                gla_iteration(h, NG - 1, 2, last=True)
                R = h * HEADS + (HEADS - 1)
                pe.wait_ge(pT_hi, h * 2 + 2)
                pe.wait_ge(pT_lo, h * 2 + 2)
                hooks = {1: lambda: level(R, 5), 4: lambda: level(R, 6), 7: lambda: readout(R, 2)}
                for e in range(E_TILES):
                    s, par, o = I_SLABS + e // 8, e % 2, E_TILE + e
                    if e % 8 == 0:
                        pe.wait_ge(w_hi_ready, (h * SLABS + s) * 2 + 2)
                        pe.wait_ge(w_lo_ready, (h * SLABS + s) * 2 + 4)
                    pe.wait_ge(acc_free[par], h * (TILES // 2) + (o // 2 + 1))
                    cols = slice((e % 8) * P, (e % 8 + 1) * P)
                    for k in range(2):
                        last = passes(acc[par][:, :], w_hi[s % 2][:, k, cols], w_lo[s % 2][:, k, cols],
                                      act_hi[:, KT - 2 + k, :], act_lo[:, KT - 2 + k, :], k == 0, k == 1)
                    last.then_inc(acc_ready, 1)
                    if e in hooks:
                        hooks[e]()

                def e_rows():
                    pe.wait_ge(y_ready, h * HEADS + (HEADS + 1))
                    pe.wait_ge(e_added, h * E_TILES + E_TILES)
                    nc.tensor.matmul(ms_ps[:, :], ones[:, :], sq_sum[:, :], start=True, stop=True).then_inc(rows_ready, 1)

                def o_pair(i, first=False, last=False):
                    for par in range(2):
                        c = i * 2 + par

                        hooks = {}
                        if first and par == 0:
                            hooks[1] = lambda: o_transpose(R, 2)
                            hooks[8] = e_rows
                        slab(h, c + O_SLAB, par, i + O_TILE // 2, hooks,
                             KT if (first and par == 0) else None, last and par == 1)

                o_pair(0, True)
                with pe.Fori(1, KT // 2 - 1) as i:
                    o_pair(i)
                o_pair(KT // 2 - 1, last=True)
                def g_pair(i, first=False, last=False):
                    for par in range(2):
                        hooks = {}
                        if first and par == 0:
                            def h_rows():
                                pe.wait_ge(h_added, h * KT + KT)
                                pe.wait_ge(rvar_ready, h * 2 + 1)
                                nc.tensor.matmul(ms_ps[:, :], ones[:, :], sq_sum[:, :], start=True,
                                                 stop=True).then_inc(rows_ready, 1)
                            hooks = {11: h_rows}
                        if last and par == 1 and h < HALVES - 1:
                            hooks = {k + 10: (lambda k=k: transpose_x(h + 1, k)) for k in range(len(ring))}
                        slab(h, i * 2 + (G_SLAB + par), par, i + G_TILE // 2, hooks,
                             2 * KT if (first and par == 0) else None, last and par == 1)

                g_pair(0, True)
                with pe.Fori(1, KT // 2 - 1) as i:
                    g_pair(i)
                g_pair(KT // 2 - 1, last=True)
            row_sums(HALVES - 1)

        @block.scalar
        def _(act):
            st = Steps(act, act_steps, lambda: nc.scalar.copy(act_dummy[:, :], vecs[:, 0:1]))
            A = nc.scalar.activation
            act.preload_act_table_set("natural_log_exp_and_others")

            def split_weights(h, s, par, prev_tile, js=(0, 1)):
                act.wait_ge(acc_ready, h * TILES + (prev_tile + 3))
                g = h * SLABS + s
                for j in js:
                    act.wait_ge(raw_loaded[j], g * 16 + 16)
                    nc.scalar.copy(w_hi[par][:, j, :], w_raw[j][:, :]).then_inc(w_hi_ready, 1)

            def softplus(h, no, src, ready_sem, ready_val, bias=None):
                act.wait_ge(ready_sem, ready_val)
                act.wait_ge(ls_ready, h * SIGS + (no + 1))
                st.mark(A(t1, src, ACT.Abs) if bias is None else A(t1, src, ACT.Abs, bias=bias))
                st.wait()
                st.mark(A(t1, t1, ACT.Exp, scale=-1.0))
                st.wait()
                A(t1, t1, ACT.Ln, bias=1.0).then_inc(sp_ready, 1)

            def sigmoid(h, no):
                act.wait_ge(ls_ready, h * SIGS + (no + 2))
                A(t2, t2, ACT.Exp).then_inc(sig_ready, 1)

            def wait_act_free(h, stage_no, k):
                if k % 4 == 0:
                    if k < 12:
                        act.wait_ge(act_free, h * 10 + stage_no * 3 + (k // 4 + 2))
                    else:
                        act.wait_ge(acc_ready, tile_done(h, (E_TILE, G_TILE, TILES)[stage_no] - 1))

            def p_high(h):
                act.wait_ge(act_free, h * 10 + 1)
                act.wait_ge(p_loaded, h * 16 + 16)
                for k in range(2):
                    nc.scalar.copy(act_hi[:, KT - 2 + k, :], p_raw[:, k * TH:(k + 1) * TH]).then_inc(pT_hi, 1)

            def y_high(h, k):
                wait_act_free(h, 0, k)
                nc.scalar.copy(act_hi[:, k, :], feat[:, k, :]).then_inc(act_hi_ready, 1)

            def rec_decays(R):
                act.wait_ge(kt_arg, R + 1)
                A(kt, kt, ACT.Exp).then_inc(kt_exp, 1)
                A(qb, b_t, ACT.Exp).then_inc(qb_exp, 1)
                A(e_last, b_t[:, C - 1:TH:C], ACT.Exp).then_inc(elast_ready, 1)

            def rec_level(R, l):
                act.wait_ge(lv_arg, R * LEVELS + (l + 1))
                A(x_lv[l % 2], x_lv[l % 2], ACT.Exp).then_inc(lv_exp, 1)

            def k_copy(R):
                act.wait_ge(kttr_ready, R + 1)
                nc.scalar.copy(kt_pos, tr_ps[:, :]).then_inc(ktpos_ready, 1)
                act.wait_ge(dgps_ready, R + 1)
                nc.scalar.copy(diag, ms_ps[:, 0:NC_]).then_inc(dg_ready, 1)

            def v_copy_feat(h, o, par, vb):
                act.wait_ge(acc_ready, tile_done(h, o))
                A(v_feat[:, vb * TH:(vb + 1) * TH], acc[par][:, :], ACT.Copy).then_inc(acc_free[par], 1)

            def v_copy(R, nb):
                act.wait_ge(vtr_ready, R + 1)
                v = v_pos[:, 0:NC_ * nb * P].rearrange("p (c b n) -> p c b n", b=nb, n=P)
                for vb in range(nb):
                    ins = nc.scalar.copy(v[:, :, vb, :], (tr_ps, ms_ps)[vb][:, :].rearrange("p (c n) -> p c n", n=P))
                    ins.then_inc(v_ready, 1) if vb == nb - 1 else st.mark(ins)

            def o_rsqrt(R):
                act.wait_ge(ovar_ready, R + 1)
                st.mark(A(o_tmp, o_var, ACT.Ln))
                st.wait()
                A(o_r, o_tmp, ACT.Exp, scale=-0.5).then_inc(oy0_ready, 1)

            def o_squares(R, nb, then_rsqrt=True):
                act.wait_ge(o_copied, R + 2)
                for c in range(NC_):
                    ins = A(junk[:, c * nb * P:(c + 1) * nb * P], on_pos[:, c * nb * P:(c + 1) * nb * P],
                            ACT.Square, accum_out=o_ss[:, c:c + 1])
                    ins.then_inc(oss_ready, 1) if c == NC_ - 1 else st.mark(ins)
                if then_rsqrt:
                    o_rsqrt(R)

            def f_gate(h, n):
                softplus(h, n * 3, acc[1][:, :], acc_ready, tile_done(h, n * SLABS_H + 1))
                sigmoid(h, n * 3)
                act.wait_ge(f_ready, h * NH + (n + 1))
                A(t2, t2, ACT.Ln).then_inc(g_ready, 1)

            def hgrn_iteration(h, n):
                r0 = h * HEADS + n
                R = r0 - 1
                s = n * SLABS_H
                sg = n * 3
                rec_decays(R)
                split_weights(h, s + 1, 1, s - 1)
                rec_level(R, 0)
                softplus(h, sg - 1, acc[1][:, :], acc_ready, tile_done(h, s - 1))
                sigmoid(h, sg - 1)
                k_copy(R)
                rec_level(R, 1)
                split_weights(h, s + 2, 0, s)
                v_copy_feat(h, s, 0, 0)
                for l in (2, 3):
                    rec_level(R, l)
                for l in (4, 5):
                    rec_level(R, l)
                split_weights(h, s + 3, 1, s + 1)
                rec_level(R, 6)
                f_gate(h, n)
                split_weights(h, s + 4, 0, s + 2)
                o_squares(R, 1)
                softplus(h, sg + 1, acc[0][:, :], acc_ready, tile_done(h, s + 2))
                sigmoid(h, sg + 1)
                v_copy(r0, 1)

            def gla_iteration(h, m, rec_nb, last=False):
                r0 = h * HEADS + (m + NH)
                R = r0 - 1
                s = m * SLABS_G + NH * SLABS_H
                sg = m * 3 + 3 * NH
                rec_decays(R)
                split_weights(h, s + 1, 1, s - 1)
                rec_level(R, 0)
                softplus(h, sg - 1, acc[1][:, :], acc_ready, tile_done(h, s - 1))
                sigmoid(h, sg - 1)
                k_copy(R)
                rec_level(R, 1)
                split_weights(h, s + 2, 0, s)
                v_copy_feat(h, s, 0, 0)
                for l in (2, 3, 4):
                    rec_level(R, l)
                split_weights(h, s + 3, 1, s + 1)
                rec_level(R, 5)
                v_copy_feat(h, s + 1, 1, 1)
                rec_level(R, 6)
                split_weights(h, s + 4, 0, s + 2)
                act.wait_ge(hv_ready, r0 + 1)
                softplus(h, sg, ms_ps[:, :], logit_ready, h * NG + (m + 1), bias=hv_now[:, 0:1])
                split_weights(h, s + 5, 1, s + 3)
                o_squares(R, rec_nb)
                if last:
                    rec_decays(r0)
                    rec_level(r0, 0)
                    rec_level(r0, 1)
                    rec_level(r0, 2)
                    v_copy(r0, 2)
                split_weights(h, s + 6, 0, s + 4)
                if last:
                    rec_level(r0, 3)
                    k_copy(r0)
                softplus(h, sg + 1, acc[0][:, :], acc_ready, tile_done(h, s + 4))
                sigmoid(h, sg + 1)
                if last:
                    act.wait_ge(y_ready, r0 + 1)
                    for k in range(4):
                        y_high(h, k)
                    rec_level(r0, 4)
                    for k in range(4, 8):
                        y_high(h, k)
                    p_high(h)
                    for k in range(8, 12):
                        y_high(h, k)
                else:
                    v_copy(r0, 2)

            ring = [lv_ps[0], lv_ps[1], so_ps[0], so_ps[1], tr_ps]

            def x_square(c, last):
                st.wait()
                ins = A(ms_ps[:, :], work[:, bass.ds(c, 1), :].rearrange("p o n -> p (o n)"), ACT.Square,
                        accum_out=x_ss[:, bass.ds(c, 1)])
                ins.then_inc(xss_ready, 1) if last else st.mark(ins)

            def x_rsqrt(no, ts=slice(0, 4)):
                act.wait_ge(xvar_ready, no + 1)
                st.mark(A(x_tmp[:, ts], x_var[:, ts], ACT.Ln))
                st.wait()
                A(x_r[:, ts], x_tmp[:, ts], ACT.Exp, scale=-0.5).then_inc(xy0_ready, 1)

            def g_gate(h, i, par):
                no = i * 2 + (3 * HEADS + par)
                softplus(h, no, g_t, g_arg, h * KT + (i * 2 + par + 1))
                sigmoid(h, no)
                act.wait_ge(g2_sum, h * KT + (i * 2 + par + 1))
                A(t1, g_t, ACT.Square).then_inc(g2_sq, 1)

            def f_rsqrt(h):
                act.wait_ge(fvar_ready, h + 1)
                st.mark(A(f_y0, f_var, ACT.Ln))
                st.wait()
                A(f_y0, f_y0, ACT.Exp, scale=-0.5).then_inc(fy0_ready, 1)

            for t in range(4):
                act.wait_ge(x_loaded[t], 16)
                for a in range(4):
                    if (t, a) == (3, 2):
                        act.wait_ge(x_end_loaded, 16)
                    if a == 0 and t:
                        act.wait_ge(xss_ready, t)
                    x_square(t * 4 + a, a == 3)
                    if a == 0 and t:
                        x_rsqrt(t - 1, slice(t - 1, t))
            x_rsqrt(3, slice(3, 4))
            split_weights(0, 0, 0, -2)
            act.wait_ge(first_loaded, 16 * 2)
            st.fresh()
            for h in range(HALVES):
                for k in range(KT):
                    if h:
                        wait_act_free(h - 1, 2, k)
                    act.wait_ge(xt_ready, h * KT + (k + 1))
                    A(act_hi[:, k, :], ring[k % 5][:, :], ACT.Copy, scale=nmix[:, k:k + 1]).then_inc(act_hi_ready, 1)
                split_weights(h, 1, 1, -1)
                if h == 0:
                    act.wait_ge(glrw_loaded, 16)
                    nc.scalar.copy(glr_w[:, :, 0:RANK], glr_raw.rearrange("p (k n) -> p k n", n=RANK)
                                   ).then_inc(glrw_hi, 1)
                    act.wait_ge(lb_arg, 1)
                    A(lb_t[:, :, :], lb_t[:, :, :], ACT.Exp).then_inc(lb_exp, 1)
                else:
                    g_gate(h - 1, KT // 2 - 1, 1)
                split_weights(h, 2, 0, 0)
                if h:
                    f_rsqrt(h - 1)
                v_copy_feat(h, 0, 0, 0)
                act.wait_ge(glr_ready, h + 1)
                nc.scalar.copy(glr_t[0:2 * RANK, :], ms_ps[0:2 * RANK, :]).then_inc(glrt_ready, 1)
                split_weights(h, 3, 1, 1)
                f_gate(h, 0)
                split_weights(h, 4, 0, 2)
                softplus(h, 1, acc[0][:, :], acc_ready, tile_done(h, 2))
                sigmoid(h, 1)
                v_copy(h * HEADS, 1)
                st.fresh()
                with act.Fori(1, NH) as n:
                    hgrn_iteration(h, n)
                    st.fresh()
                gla_iteration(h, 0, 1)
                st.fresh()
                with act.Fori(1, NG - 1) as m:
                    gla_iteration(h, m, 2)
                    st.fresh()
                gla_iteration(h, NG - 1, 2, last=True)
                st.fresh()
                R = h * HEADS + (HEADS - 1)
                sg = 3 * HEADS - 1
                rec_level(R, 5)
                for e in range(E_TILES):
                    par = e % 2
                    act.wait_ge(acc_ready, tile_done(h, E_TILE + e))
                    if e >= 2:
                        act.wait_ge(e_stored[par], h * 128 + 16 * (e // 2))
                        act.wait_ge(e_added, h * E_TILES + (e - 1))
                    A(sq_e[par], acc[par][:, :], ACT.Square).then_inc(e_sq, 1)
                    nc.scalar.copy(e_buf[par], acc[par][:, :]).then_inc(acc_free[par], 1)
                    if e == 1:
                        rec_level(R, 6)
                    if e in (1, 2):
                        split_weights(h, I_SLABS + 1, 1, I_SLABS - 1, (e - 1,))
                    if e in (3, 4, 5):
                        if e == 3:
                            act.wait_ge(acc_free[1], tile_free(h, (I_SLABS - 1) // 2))
                            act.wait_ge(ls_ready, h * SIGS + (sg + 1))
                            st.mark(A(t1, z_last, ACT.Abs))
                        elif e == 4:
                            st.wait()
                            st.mark(A(t1, t1, ACT.Exp, scale=-1.0))
                        else:
                            st.wait()
                            A(t1, t1, ACT.Ln, bias=1.0).then_inc(sp_ready, 1)
                    if e == 6:
                        sigmoid(h, sg)
                    if e in y_high_at:
                        y_high(h, y_high_at[e])
                    if e in (9, 10):
                        split_weights(h, O_SLAB, 0, E_TILE + 7, (e - 9,))
                    if e == 11:
                        o_squares(R, 2, False)
                    if e == 12:
                        o_rsqrt(R)
                st.fresh()
                act.wait_ge(y_ready, h * HEADS + (HEADS + 1))
                act.wait_ge(acc_ready, tile_done(h, O_TILE - 1))
                for k in range(KT - 2, KT):
                    nc.scalar.copy(act_hi[:, k, :], feat[:, k, :]).then_inc(act_hi_ready, 1)

                def h_square(i, par):
                    act.wait_ge(acc_free[par], tile_free(h, i + O_TILE // 2))
                    A((t1, t2)[par], h_sb[par], ACT.Square).then_inc(h_sq, 1)

                def o_split(i, par):
                    split_weights(h, i * 2 + (O_SLAB + 1 + par), 1 - par, i * 2 + (O_TILE - 1 + par))

                def split_h(k):
                    wait_act_free(h, 1, k)
                    act.wait_ge(h1_ready, h * KT + min(k + 1, KT))
                    A(act_hi[:, k, :], feat[:, k, :], ACT.Copy, scale=pgn[:, k:k + 1]).then_inc(act_hi_ready, 1)

                o_split(0, 0)
                rv = h * 2 + 1
                act.wait_ge(rvar_ready, rv)
                st.mark(A(t2, t1, ACT.Ln))
                st.wait()
                A(t2, t2, ACT.Exp, scale=-0.5).then_inc(ry0_ready, 1)
                st.fresh()

                with act.Fori(0, KT // 2 - 1) as i:
                    for par in range(2):
                        o_split(*((i, 1) if par == 0 else (i + 1, 0)))
                        h_square(i, par)
                o_split(KT // 2 - 1, 1)
                h_square(KT // 2 - 1, 0)
                for k in range(8):
                    split_h(k)
                for k in range(8, 12):
                    split_h(k)
                h_square(KT // 2 - 1, 1)
                for k in range(12, KT):
                    split_h(k)

                def g_split(i, par):
                    split_weights(h, i * 2 + (G_SLAB + 1 + par), 1 - par, i * 2 + (G_TILE - 1 + par))

                g_split(0, 0)
                act.wait_ge(rvar_ready, rv + 1)
                st.mark(A(t2, t1, ACT.Ln))
                st.wait()
                A(t2, t2, ACT.Exp, scale=-0.5).then_inc(ry0_ready, 1)
                st.fresh()

                more = h < HALVES - 1

                def g_pair(i, squares=False, last_squares=False):
                    for par in range(2):
                        g_split(*((i, 1) if par == 0 else (i + 1, 0)))
                        g_gate(h, i, par)
                        if squares:
                            for a in range(2):
                                x_square(i * 4 + (par * 2 + a - 8), last_squares and (par, a) == (1, 1))

                with act.Fori(0, 2) as i:
                    g_pair(i)
                    st.fresh()
                if more:
                    for t in range(4):
                        act.wait_ge(x_loaded[t], (h + 1) * 16 + 16)
                with act.Fori(2, 5) as i:
                    g_pair(i, more)
                    st.fresh()
                g_pair(5, more, True)
                if more:
                    x_rsqrt(h + 4)
                g_pair(6)
                if more:
                    g_split(7, 1)
                g_gate(h, 7, 0)
                st.fresh()
            g_gate(HALVES - 1, KT // 2 - 1, 1)
            f_rsqrt(HALVES - 1)

        @block.vector
        def _(vec_e):
            v = nc.vector
            st = Steps(vec_e, vec_steps, lambda: v.memset(vec_dummy[:, :], 0.0))

            def newton(r, y0, var, tmp):
                st.mark(v.tensor_tensor(tmp, y0, y0, ALU.mult))
                st.wait()
                st.mark(v.tensor_tensor(tmp, tmp, var, ALU.mult))
                st.wait()
                st.mark(v.tensor_scalar(tmp, tmp, -0.5, 1.5, ALU.mult, ALU.add))
                st.wait()
                return v.tensor_tensor(r, y0, tmp, ALU.mult)

            def log_sigmoid(h, no, src):
                vec_e.wait_ge(sp_ready, h * SIGS + (no + 1))
                st.wait()
                v.scalar_tensor_tensor(out=t2, in0=src, scalar=0.0, in1=t1, op0=ALU.min, op1=ALU.subtract
                                       ).then_inc(ls_ready, 1)

            def silu(h, sig_no, dst, src, scale, par):
                vec_e.wait_ge(sig_ready, h * SIGMOIDS + (sig_no + 1))
                v.scalar_tensor_tensor(out=dst, in0=src, scalar=scale, in1=t2, op0=ALU.mult, op1=ALU.mult
                                       ).then_inc(acc_free[par], 1)

            def rec_begin(R):
                b3 = b_t.rearrange("p (c n) -> p c n", n=C)
                st.wait()
                v.tensor_tensor(kt.rearrange("p (c n) -> p c n", n=C), b3[:, :, C - 1:C].to_broadcast([P, NC_, C]),
                                b3, ALU.subtract).then_inc(kt_arg, 1)
                v.tensor_tensor(qk, q_t, k_t, ALU.mult).then_inc(qk_ready, 1)

            def halves_of(t, l):
                b4 = t.rearrange("p (n two s) -> p n two s", two=2, s=1 << l)
                return b4[:, :, 0, :], b4[:, :, 1, :]

            def level_arg(R, l):
                s = 1 << l
                blo, bup = halves_of(b_t, l)
                xlo, xup = halves_of(x_lv[l % 2], l)
                mid = blo[:, :, s - 1:s].to_broadcast([P, TH // (2 * s), s])
                st.mark(v.tensor_tensor(xlo, mid, blo, ALU.subtract))
                v.tensor_tensor(xup, bup, mid, ALU.subtract).then_inc(lv_arg, 1)

            def level_mul(R, l):
                vec_e.wait_ge(lv_exp, R * LEVELS + (l + 1))
                xlo, xup = halves_of(x_lv[l % 2], l)
                klo, _ = halves_of(k_t, l)
                _, qup = halves_of(q_t, l)
                st.mark(v.tensor_tensor(xlo, xlo, klo, ALU.mult))
                v.tensor_tensor(xup, xup, qup, ALU.mult).then_inc(lv_in, 1)

            def mask_level(R, l):
                vec_e.wait_ge(lv_ready, R * LEVELS + (l + 1))
                s = 1 << l
                st.space()
                st.wait()
                v.copy_predicated(halves_of(attn, l)[1], mask_sb[:, l, :].rearrange("p (n s) -> p n s", s=s),
                                  lv_ps[l % 2][:, 0:TH // 2].rearrange("p (n s) -> p n s", s=s)
                                  ).then_inc(masked, 1)

            def decayed(R):
                vec_e.wait_ge(kt_exp, R + 1)
                v.tensor_tensor(kt, kt, k_t, ALU.mult).then_inc(kt_ready, 1)
                vec_e.wait_ge(qb_exp, R + 1)
                v.tensor_tensor(qb, qb, q_t, ALU.mult).then_inc(qb_ready, 1)

            def state_chain(R, nb, state):
                w = nb * P
                st.mark(v.tensor_copy(s_in[:, 0:w], state))
                vec_e.wait_ge(su_ready, R + 1)
                vec_e.wait_ge(elast_ready, R + 1)
                for c in range(NC_):
                    st.wait()
                    dst = s_in[:, (c + 1) * w:(c + 2) * w] if c < NC_ - 1 else state
                    ps = so_ps[(c * nb) // NC_][:, (c * nb) % NC_ * P:((c * nb) % NC_ + nb) * P]
                    ins = v.scalar_tensor_tensor(out=dst, in0=s_in[:, c * w:(c + 1) * w], scalar=e_last[:, c:c + 1],
                                                 in1=ps, op0=ALU.mult, op1=ALU.add)
                    st.mark(ins) if c < NC_ - 1 else ins.then_inc(s_ready, 1)

            def o_copy(R, nb):
                w = nb * P
                vec_e.wait_ge(o_ready, R + 1)
                vec_e.wait_ge(dg_ready, R + 1)
                for c in range(NC_):
                    ps = so_ps[(c * nb) // NC_][:, (c * nb) % NC_ * P:((c * nb) % NC_ + nb) * P]
                    ins = v.scalar_tensor_tensor(out=on_pos[:, c * w:(c + 1) * w], in0=v_pos[:, c * w:(c + 1) * w],
                                                 scalar=diag[:, c:c + 1], in1=ps, op0=ALU.mult, op1=ALU.add)
                    st.mark(ins) if c < NC_ - 1 else ins.then_inc(o_copied, 1)

            def o_variance(R, nb):
                vec_e.wait_ge(oss_ready, R + 1)
                v.tensor_scalar(o_var, o_ss, 1.0 / (nb * P), EPS, ALU.mult, ALU.add).then_inc(ovar_ready, 1)

            def o_norm(R, nb, variance=True):
                w = nb * P
                if variance:
                    o_variance(R, nb)
                vec_e.wait_ge(oy0_ready, R + 1)
                st.mark(newton(o_r, o_r, o_var, o_tmp))
                st.wait()
                for c in range(NC_):
                    ins = v.tensor_scalar(on_pos[:, c * w:(c + 1) * w], on_pos[:, c * w:(c + 1) * w],
                                          o_r[:, c:c + 1], None, ALU.mult)
                    st.mark(ins) if c < NC_ - 1 else ins.then_inc(on_ready, 1)

            def y_out(R, nb, k0, norm_col):
                vec_e.wait_ge(ontr_ready, R + 1)
                for vb in range(nb):
                    dst = feat[:, bass.ds(k0 + vb, 1), :].rearrange("p o n -> p (o n)")
                    ins = v.scalar_tensor_tensor(out=dst, in0=(tr_ps, ms_ps)[vb][:, :],
                                                 scalar=hv_rec[:, norm_col + vb:norm_col + vb + 1],
                                                 in1=zs[:, vb * TH:(vb + 1) * TH], op0=ALU.mult, op1=ALU.mult)
                    st.mark(ins) if vb < nb - 1 else ins.then_inc(y_ready, 1)

            def head_constants(r0, r, w2_m=None):
                st.wait()
                st.mark(v.tensor_copy(hv_rec[:, 0:3], hv_now[:, 0:3]))
                st.wait()
                if w2_m is not None:
                    st.mark(v.tensor_copy(w2_now[0:2 * RANK, :], w2_sb[0:2 * RANK, bass.ds(w2_m * P, P)]))
                v.tensor_copy(hv_now[:, 0:3], head_vec[:, bass.ds(r * 3, 3)]).then_inc(hv_ready, 1)

            ring = [lv_ps[0], lv_ps[1], so_ps[0], so_ps[1], tr_ps]

            def x_factors(no, ts=slice(0, 4)):
                vec_e.wait_ge(xss_ready, no + 1)
                st.mark(v.tensor_reduce(x_var[:, ts], x_ss.rearrange("p (t a) -> p t a", a=4)[:, ts, :], AX.X, ALU.add))
                st.wait()
                v.tensor_scalar(x_var[:, ts], x_var[:, ts], 1.0 / D, EPS, ALU.mult, ALU.add).then_inc(xvar_ready, 1)
                vec_e.wait_ge(xy0_ready, no + 1)
                st.mark(newton(x_r[:, ts], x_r[:, ts], x_var[:, ts], x_tmp[:, ts]))
                st.wait()

            def x_scale(t):
                v.tensor_scalar(x_in[:, t, :], x_in[:, t, :], x_r[:, t:t + 1], None, ALU.mult).then_inc(xn_ready, 1)

            def f_gate(h, n):
                log_sigmoid(h, n * 3, acc[1][:, :])
                vec_e.wait_ge(sig_ready, h * SIGMOIDS + (n * 3 + 1))
                v.tensor_scalar(t2, t2, hv_now[:, 1:2], hv_now[:, 0:1], ALU.mult, ALU.add).then_inc(acc_free[1], 1)
                vec_e.wait_ge(acc_free[1], tile_free(h, n * 2))
                st.mark(v.tensor_scalar(k_t, t2, -1.0, 1.0, ALU.mult, ALU.add))
                st.wait()
                v.tensor_scalar(t2, t2, LN_MIN, None, ALU.max).then_inc(f_ready, 1)

            def decay_sum(h, n):
                vec_e.wait_ge(g_ready, h * NH + (n + 1))
                st.mark(v.tensor_tensor_scan(b_t, restart_sb[:, :], t2, 0.0, ALU.mult, ALU.add))

            def q_gate(h, n):
                log_sigmoid(h, n * 3 + 1, acc[0][:, :])
                silu(h, n * 3 + 1, q_t, acc[0][:, :], SCALE, 0)
                vec_e.wait_ge(acc_free[0], tile_free(h, n * 2 + 1))

            def g_first(h, i, par):
                c = i * 2 + par
                gv = gv_now[:, par, :]
                st.mark(v.tensor_copy(gv[:, 0:3], g_vec[:, bass.ds(c * 3, 3)]))
                vec_e.wait_ge(acc_ready, tile_done(h, c + G_TILE))
                v.tensor_tensor(g_t, acc[par][:, :], r_h[:, :], ALU.mult).then_inc(acc_free[par], 1)
                vec_e.wait_ge(acc_free[par], tile_free(h, i + G_TILE // 2))
                v.tensor_scalar(g_t, g_t, gv[:, 0:1], None, ALU.add).then_inc(g_arg, 1)

            def g_rest(h, i, par):
                c = i * 2 + par
                gv = gv_now[:, par, :]
                vec_e.wait_ge(e_loaded[par], h * 128 + (i * 16 + 16))
                v.scalar_tensor_tensor(out=g_m, in0=e_in[par], scalar=gv[:, 1:2], in1=r_e[:, :],
                                       op0=ALU.mult, op1=ALU.mult).then_inc(e_used, 1)
                vec_e.wait_ge(e_used, h * KT + (c + 1))
                log_sigmoid(h, c + 3 * HEADS, g_t)
                vec_e.wait_ge(sig_ready, h * SIGMOIDS + (c + (3 * NH + 2 * NG + 1)))
                st.mark(v.tensor_tensor(g_m, g_m, t2, ALU.mult))
                st.wait()
                v.tensor_tensor(g_t, feat[:, bass.ds(c, 1), :].rearrange("p o n -> p (o n)"), g_m, ALU.add
                                ).then_inc(g2_sum, 1)
                vec_e.wait_ge(g2_sum, h * KT + (c + 1))
                st.mark(v.tensor_scalar(feat[:, bass.ds(c, 1), :].rearrange("p o n -> p (o n)"), g_t,
                                        gv[:, 2:3], None, ALU.mult))
                vec_e.wait_ge(g2_sq, h * KT + (c + 1))
                v.tensor_tensor(sq_sum[:, :], sq_sum[:, :], t1, ALU.add).then_inc(g2_ready, 1)
                vec_e.wait_ge(g2_ready, h * KT + (c + 1))

            def f_factors(h):
                vec_e.wait_ge(fsum_ready, h + 1)
                v.tensor_scalar(f_var, ms_ps[:, :], 1.0 / D, EPS, ALU.mult, ALU.add).then_inc(fvar_ready, 1)
                vec_e.wait_ge(fy0_ready, h + 1)
                st.mark(newton(f_r, f_y0, f_var, f_tmp))
                st.wait()

            def f_scale(h, ns):
                for n in ns:
                    v.tensor_tensor(feat[:, n, :], feat[:, n, :], f_r, ALU.mult).then_inc(f_scaled, 1)

            def rec_first(h, R, z_no, z_sig, z_dst):
                decayed(R)
                level_arg(R, 0)
                level_mul(R, 0)
                log_sigmoid(h, z_no, acc[1][:, :])
                silu(h, z_sig, z_dst, acc[1][:, :], 1.0, 1)
                level_arg(R, 1)
                level_mul(R, 1)

            def next_level(R, l):
                mask_level(R, l)
                level_arg(R, l + 2)
                level_mul(R, l + 2)

            def hgrn_iteration(h, n):
                r0 = h * HEADS + n
                R = r0 - 1
                head_constants(r0, n)
                rec_first(h, R, n * 3 - 1, n * 3 - 1, zs[:, 0:TH])
                state_chain(R, 1, state_h[:, bass.ds((n - 1) * P, P)])
                for l in range(LEVELS - 2):
                    next_level(R, l)
                vec_e.wait_ge(hv_ready, r0 + 1)
                f_gate(h, n)
                mask_level(R, LEVELS - 2)
                decay_sum(h, n)
                mask_level(R, LEVELS - 1)
                o_copy(R, 1)
                o_norm(R, 1)
                q_gate(h, n)
                y_out(R, 1, n - 1, 2)
                rec_begin(r0)

            def y_low(h, k):
                vec_e.wait_ge(act_hi_ready, h * (3 * KT) + (KT + k + 1))
                v.tensor_tensor(act_lo[:, k, :], feat[:, k, :], act_hi[:, k, :].bitcast(F32), ALU.subtract
                                ).then_inc(act_lo_ready, 1)

            def gla_iteration(h, m, rec_nb, last=False):
                r0 = h * HEADS + (m + NH)
                R = r0 - 1
                half = NH * SLABS_H // 2 + m * 3 if isinstance(m, int) else m * 3 + NH * SLABS_H // 2
                s, sg, sig = m * SLABS_G + NH * SLABS_H, m * 3 + 3 * NH, m * 2 + 3 * NH
                head_constants(r0, m + NH, m)
                zb = rec_nb - 1
                rec_first(h, R, sg - 1, sig - 1, zs[:, zb * TH:(zb + 1) * TH])
                state_chain(R, rec_nb, state_h[:, (NH - 1) * P:NH * P] if rec_nb == 1
                            else state_g[:, bass.ds((m - 1) * 2 * P, 2 * P)])
                for l in range(LEVELS - 2):
                    next_level(R, l)
                vec_e.wait_ge(lv_in, R * LEVELS + LEVELS)
                vec_e.wait_ge(acc_ready, tile_done(h, s + 2))
                v.tensor_copy(k_t, acc[0][:, :]).then_inc(acc_free[0], 1)
                for l in (LEVELS - 2, LEVELS - 1):
                    mask_level(R, l)
                vec_e.wait_ge(hv_ready, r0 + 1)
                vec_e.wait_ge(sp_ready, h * SIGS + (sg + 1))
                st.mark(v.tensor_scalar(t2, ms_ps[:, :], hv_now[:, 0:1], 0.0, ALU.add, ALU.min))
                st.wait()
                v.tensor_tensor(t2, t2, t1, ALU.subtract).then_inc(ls_ready, 1)
                vec_e.wait_ge(ls_ready, h * SIGS + (sg + 2))
                st.mark(v.tensor_tensor_scan(b_t, restart_sb[:, :], t2, 0.0, ALU.mult, ALU.add))
                st.wait()
                st.mark(v.tensor_scalar(b_t, b_t, 1.0 / TAU, None, ALU.mult))
                vec_e.wait_ge(acc_ready, tile_done(h, s + 3))
                v.tensor_scalar(q_t, acc[1][:, :], SCALE, None, ALU.mult).then_inc(acc_free[1], 1)
                o_copy(R, rec_nb)
                o_norm(R, rec_nb)
                if last:
                    vec_e.wait_ge(acc_free[1], tile_free(h, half + 1))
                    rec_begin(r0)
                    decayed(r0)
                    level_arg(r0, 0)
                    level_mul(r0, 0)
                y_out(R, rec_nb, NH - 1 if rec_nb == 1 else (m - 1) * 2 + NH, 2 if rec_nb == 1 else 1)
                if last:
                    level_arg(r0, 1)
                    level_mul(r0, 1)
                    next_level(r0, 0)
                    next_level(r0, 1)
                log_sigmoid(h, sg + 1, acc[0][:, :])
                vec_e.wait_ge(y_ready, R + 2)
                silu(h, sig, zs[:, 0:TH], acc[0][:, :], 1.0, 0)
                vec_e.wait_ge(acc_free[0], tile_free(h, half + 2))
                if last:
                    for k in range(4):
                        y_low(h, k)
                    next_level(r0, 2)
                    for k in range(4, 6):
                        y_low(h, k)
                else:
                    rec_begin(r0)

            def constants():
                vec_e.wait_ge(const_loaded, 16 * 4)
                st.mark(v.tensor_copy(mask_sb[:, :, :],
                                      mask_f32.rearrange("p (l n) -> p l n", l=LEVELS)))
                vec_e.wait_ge(glrw_hi, 1)
                v.tensor_tensor(glr_w[:, :, RANK:2 * RANK], glr_raw.rearrange("p (k n) -> p k n", n=RANK),
                                glr_w[:, :, 0:RANK].bitcast(F32), ALU.subtract).then_inc(glrw_ready, 1)
                st.mark(v.tensor_tensor(lb_t[:, 0, :], lb_sb[:, 0, :], lb_sb[:, 1, :], ALU.max))
                st.wait()
                st.mark(v.tensor_tensor(lb_t[:, 1, :], lb_sb[:, 1, :], lb_t[:, 0, :], ALU.subtract))
                st.wait()
                v.tensor_tensor(lb_t[:, 0, :], lb_sb[:, 0, :], lb_t[:, 0, :], ALU.subtract).then_inc(lb_arg, 1)
                vec_e.wait_ge(lb_exp, 1)
                st.mark(v.tensor_tensor(lb_sb[:, 0, :], lb_t[:, 0, :], lb_t[:, 1, :], ALU.add))
                st.wait()
                st.mark(v.reciprocal(lb_sb[:, 1, :], lb_sb[:, 0, :]))
                st.wait()
                hvec = head_vec.rearrange("p (r n) -> p r n", n=3)
                st.mark(v.tensor_tensor(hvec[:, 0:NH, 0], lb_t[:, 0, :], lb_sb[:, 1, :], ALU.mult))
                st.wait()
                st.mark(v.tensor_scalar(hvec[:, 0:NH, 1], hvec[:, 0:NH, 0], -1.0, 1.0, ALU.mult, ALU.add))
                st.mark(v.memset(hv_now[:, :], 0.0))

            st.mark(v.memset(state_h[:, :], 0.0))
            st.mark(v.memset(state_g[:, :], 0.0))
            v.memset(ones[:, :], 1.0).then_inc(const_ready, 1)
            vec_e.wait_ge(const_ready, 1)
            st.mark(v.tensor_copy(glr_all[:, KT * 2 * RANK:], ones[:, 0:P - 2 * RANK]))
            for t in range(4):
                x_factors(t, slice(t, t + 1))
                x_scale(t)
            st.fresh()
            for h in range(HALVES):
                for k in range(KT):
                    vec_e.wait_ge(act_hi_ready, h * (3 * KT) + (k + 1))
                    v.scalar_tensor_tensor(out=act_lo[:, k, :], in0=ring[k % 5][:, :], scalar=nmix[:, k:k + 1],
                                           in1=act_hi[:, k, :].bitcast(F32), op0=ALU.mult, op1=ALU.subtract
                                           ).then_inc(act_lo_ready, 1)
                if h:
                    g_first(h - 1, KT // 2 - 1, 1)
                    g_rest(h - 1, KT // 2 - 1, 1)
                else:
                    constants()
                st.mark(v.memset(attn, 0.0))
                head_constants(h * HEADS, 0)
                if h:
                    f_factors(h - 1)
                    f_scale(h - 1, range(8))
                vec_e.wait_ge(hv_ready, h * HEADS + 1)
                f_gate(h, 0)
                if h:
                    f_scale(h - 1, range(8, 12))
                decay_sum(h, 0)
                if h:
                    f_scale(h - 1, range(12, 16))
                q_gate(h, 0)
                if h:
                    vec_e.wait_ge(out_stored, h * KT * 16)
                rec_begin(h * HEADS)
                st.fresh()
                with vec_e.Fori(1, NH) as n:
                    hgrn_iteration(h, n)
                    st.fresh()
                gla_iteration(h, 0, 1)
                st.fresh()
                with vec_e.Fori(1, NG - 1) as m:
                    gla_iteration(h, m, 2)
                    st.fresh()
                gla_iteration(h, NG - 1, 2, last=True)
                R = h * HEADS + (HEADS - 1)
                st.mark(v.tensor_copy(hv_rec[:, 0:3], hv_now[:, 0:3]))
                for k in range(2):
                    vec_e.wait_ge(pT_hi, h * 2 + (k + 1))
                    v.tensor_tensor(act_lo[:, KT - 2 + k, :], p_raw[:, k * TH:(k + 1) * TH],
                                    act_hi[:, KT - 2 + k, :].bitcast(F32), ALU.subtract).then_inc(pT_lo, 1)
                vec_e.wait_ge(acc_ready, tile_done(h, I_SLABS - 1))
                vec_e.wait_ge(y_ready, R + 1)
                v.tensor_copy(z_last, acc[1][:, :]).then_inc(acc_free[1], 1)
                next_level(R, 3)
                st.mark(v.memset(sq_sum[:, :], 0.0))
                for e in range(E_TILES):
                    vec_e.wait_ge(e_sq, h * E_TILES + (e + 1))
                    if e:
                        vec_e.wait_ge(e_added, h * E_TILES + e)
                    else:
                        st.wait()
                    v.tensor_tensor(sq_sum[:, :], sq_sum[:, :], sq_e[e % 2], ALU.add).then_inc(e_added, 1)
                    if e == 0:
                        mask_level(R, 4)
                        level_arg(R, 6)
                    if e == 1:
                        level_mul(R, 6)
                    if e == 3:
                        state_chain(R, 2, state_g[:, (NG - 1) * 2 * P:NG * 2 * P])
                    if e in (2, 5):
                        mask_level(R, LEVELS - 2 + (e == 5))
                    if e == 5:
                        log_sigmoid(h, 3 * HEADS - 1, z_last)
                    if e == 7:
                        vec_e.wait_ge(sig_ready, h * SIGMOIDS + (3 * NH + 2 * NG))
                        st.mark(v.tensor_tensor(z_last, z_last, t2, ALU.mult))
                    if e == 10:
                        o_copy(R, 2)
                    if e == 11:
                        o_variance(R, 2)
                    if e == 12:
                        o_norm(R, 2, False)
                    if e in y_low_at:
                        y_low(h, y_low_at[e])
                y_out(R, 2, 2 * (NG - 1) + NH, 1)
                for k in range(KT - 2, KT):
                    y_low(h, k)

                def row_factors(no, dst):
                    vec_e.wait_ge(rows_ready, no)
                    v.tensor_scalar(t1, ms_ps[:, :], 1.0 / D, EPS, ALU.mult, ALU.add).then_inc(rvar_ready, 1)
                    st.mark(v.memset(sq_sum[:, :], 0.0))
                    vec_e.wait_ge(ry0_ready, no)
                    st.mark(newton(dst, t2, t1, g_t))
                    st.wait()

                row_factors(h * 2 + 1, r_e[:, :])
                st.fresh()
                def h_tile(i, par):
                    c = i * 2 + par
                    vec_e.wait_ge(acc_ready, tile_done(h, c + O_TILE))
                    vec_e.wait_ge(xb_loaded[par], h * 128 + (i * 16 + 16))
                    v.tensor_tensor(h_sb[par], acc[par][:, :], xt_sb[par], ALU.add).then_inc(acc_free[par], 1)
                    vec_e.wait_ge(acc_free[par], tile_free(h, i + O_TILE // 2))
                    v.tensor_copy(feat[:, bass.ds(c, 1), :].rearrange("p o n -> p (o n)"), h_sb[par]
                                  ).then_inc(h1_ready, 1)
                    vec_e.wait_ge(h_sq, h * KT + (c + 1))
                    v.tensor_tensor(sq_sum[:, :], sq_sum[:, :], (t1, t2)[par], ALU.add).then_inc(h_added, 1)
                    vec_e.wait_ge(h_added, h * KT + (c + 1))

                def h_low(k):
                    vec_e.wait_ge(act_hi_ready, h * (3 * KT) + (2 * KT + k + 1))
                    v.scalar_tensor_tensor(out=act_lo[:, k, :], in0=feat[:, k, :], scalar=pgn[:, k:k + 1],
                                           in1=act_hi[:, k, :].bitcast(F32), op0=ALU.mult, op1=ALU.subtract
                                           ).then_inc(act_lo_ready, 1)

                with vec_e.Fori(0, KT // 2 - 1) as i:
                    for par in range(2):
                        h_tile(i, par)
                h_tile(KT // 2 - 1, 0)
                for k in range(12):
                    h_low(k)
                h_tile(KT // 2 - 1, 1)
                for k in range(12, KT):
                    h_low(k)
                row_factors(h * 2 + 2, r_h[:, :])
                st.fresh()

                def g_tile(i, par):
                    g_first(h, i, par)
                    g_rest(h, i, par)

                with vec_e.Fori(0, 6) as i:
                    for par in range(2):
                        g_tile(i, par)
                    st.fresh()
                if h < HALVES - 1:
                    x_factors(h + 4)
                for i, par in ((6, 0), (6, 1), (7, 0)):
                    g_tile(i, par)
                    if h < HALVES - 1 and i == 6:
                        x_scale(par * 2)
                        x_scale(par * 2 + 1)
                st.fresh()
            g_first(HALVES - 1, KT // 2 - 1, 1)
            g_rest(HALVES - 1, KT // 2 - 1, 1)
            f_factors(HALVES - 1)
            f_scale(HALVES - 1, range(KT))


def level_masks():
    j = np.arange(C)[:, None]
    out = np.zeros((C, LEVELS, NC_, C // 2), np.float32)
    for l in range(LEVELS):
        s = 1 << l
        u = np.arange(C // 2)[None, :]
        block = u // s
        out[:, l, :, :] = ((j // (2 * s) == block) & (j % (2 * s) < s))[:, None, :]
    return out.reshape(C, LEVELS * NC_ * C // 2)


def kernel(**inputs):
    import concourse.bacc as bacc
    from concourse.bass_utils import run_bass_kernel_spmd

    a = {k: np.asarray(v) for k, v in inputs.items()}
    w_in = a["w_in"][0]

    def slab_of(w, c0):
        return w[:, c0:c0 + P].reshape(2, KT // 2, P, P).transpose(0, 2, 1, 3).reshape(2, P, 1024)

    ple = a["ple_proj"][0].reshape(2, P, 2, 1024)
    slabs = np.stack([slab_of(w_in, c) for c in slab_columns()]
                     + [ple[:, :, e, :] for e in range(2)]
                     + [slab_of(a["w_out"][0], c * P) for c in range(KT)]
                     + [slab_of(a["ple_gate_w"][0], c * P) for c in range(KT)])

    def by_tile(w):
        return w.reshape(-1, P).T

    head_vec = np.zeros((P, HEADS, 3), np.float32)
    head_vec[:, :NH, 2] = by_tile(a["hgrn_norm_w"][0])
    head_vec[:, NH:, 0] = by_tile(a["gla_gate_b"][0])
    head_vec[:, NH:, 1:] = by_tile(a["gla_norm_w"][0]).reshape(P, NG, 2)
    g_vec = np.stack([by_tile(a["ple_gate_b"][0]), by_tile(a["ple_norm_w"][0]), by_tile(a["final_norm_w"])], axis=2)
    vec = np.concatenate([by_tile(a["norm_mix_w"][0]), by_tile(a["ple_gate_norm_w"][0]),
                          head_vec.reshape(P, -1), g_vec.reshape(P, -1)], axis=1)
    restart = np.ones((P, TH), np.float32)
    restart[:, ::C] = 0.0
    arrays = {
        "x": a["x"].reshape(HALVES, 4, P, D),
        "x_feat": a["x"].reshape(HALVES, TH, KT, P).transpose(0, 2, 3, 1),
        "p": a["p"].reshape(HALVES, TH, 2, P).transpose(0, 3, 2, 1).reshape(HALVES, P, 2 * TH),
        "slabs": slabs,
        "w_glr": w_in[:, -RANK:].reshape(KT, P, RANK).transpose(1, 0, 2).reshape(P, KT * RANK),
        "w2": np.concatenate([a["gla_gate_w2"][0]] * 2, axis=0),
        "vec": vec,
        "lb_rows": a["hgrn_lb"].reshape(2, NH, P).transpose(2, 0, 1),
        "masks": level_masks(),
        "restart": restart,
        "ident": np.eye(P, dtype=np.float32),
    }
    arrays = {k: np.ascontiguousarray(v) for k, v in arrays.items()}
    nc = bacc.Bacc("TRN2", target_bir_lowering=False, num_devices=1)
    aps = [nc.dram_tensor(f"in_{k}", v.shape, mybir.dt.from_np(v.dtype), kind="ExternalInput").ap() for k, v in arrays.items()]
    out = nc.dram_tensor("out", (HALVES, KT, P, TH), F32, kind="ExternalOutput").ap()
    e_scratch = nc.dram_tensor("e_scratch", (E_TILES, P, TH), F32, kind="Internal").ap()
    build(nc, *aps, out, e_scratch)
    r = run_bass_kernel_spmd(nc, [{f"in_{k}": v for k, v in arrays.items()}], core_ids=[0])
    return r.results[0]["out"].transpose(0, 3, 1, 2).reshape(1, SEQ, D)
```
